# Optimizing a Trainium2 kernel written in Bass

```python
import math
import jax, jax.numpy as jnp
from jax import lax
import numpy as np

D_MODEL = 1024
BATCH = 1
SEQ = 512
DEPTH = 1

HEAD_DIM = 64
FOX_HEADS = 8
SWA_Q_HEADS = 8
SWA_KV_HEADS = 2
SWA_GROUP = SWA_Q_HEADS // SWA_KV_HEADS
WINDOW = 128
Q_BLOCK = 128
ROPE_THETA = 10000.0
D_FF = -(-8 * D_MODEL // (3 * 256)) * 256
DEEPNORM_ALPHA = (2 * DEPTH) ** 0.25
DEEPNORM_BETA = (8 * DEPTH) ** -0.25
LN_EPS = 1e-5

FOX_W = FOX_HEADS * HEAD_DIM
SWA_QW = SWA_Q_HEADS * HEAD_DIM
SWA_KVW = SWA_KV_HEADS * HEAD_DIM
IN_COLS = 3 * FOX_W + FOX_HEADS + SWA_QW + 2 * SWA_KVW + 2 * D_MODEL

kernel_name = "fox_swa_sink_gated_hybrid_deepnorm"

def layer_norm(x, g, b):
    xf = x.astype(jnp.float32)
    mu = jnp.mean(xf, axis=-1, keepdims=True)
    var = jnp.mean(jnp.square(xf - mu), axis=-1, keepdims=True)
    y = (xf - mu) * lax.rsqrt(var + LN_EPS)
    return (y * g.astype(jnp.float32) + b.astype(jnp.float32)).astype(x.dtype)

def apply_rope(x, pos):
    half = x.shape[-1] // 2
    inv_freq = ROPE_THETA ** (-jnp.arange(0, half, dtype=jnp.float32) / half)
    ang = pos[:, None] * inv_freq[None, :]
    cos = jnp.cos(ang)[None, :, None, :]
    sin = jnp.sin(ang)[None, :, None, :]
    xf = x.astype(jnp.float32)
    x1, x2 = xf[..., :half], xf[..., half:]
    out = jnp.concatenate([x1 * cos - x2 * sin, x2 * cos + x1 * sin], axis=-1)
    return out.astype(x.dtype)

def forgetting_attention(q, k, v, log_f):
    B, S, H, dh = q.shape
    nb = S // Q_BLOCK
    scale = 1.0 / math.sqrt(dh)
    c = jnp.cumsum(log_f, axis=1)
    cT = jnp.transpose(c, (0, 2, 1))
    qb = jnp.transpose(q.reshape(B, nb, Q_BLOCK, H, dh), (1, 0, 2, 3, 4))
    cb = jnp.transpose(c.reshape(B, nb, Q_BLOCK, H), (1, 0, 3, 2))
    kpos = jnp.arange(S)

    def one_block(args):
        qi, ci, i = args
        s = jnp.einsum('bqhd,bkhd->bhqk', qi, k, preferred_element_type=jnp.float32) * scale
        bias = ci[..., :, None] - cT[:, :, None, :]
        qpos = i * Q_BLOCK + jnp.arange(Q_BLOCK)
        mask = kpos[None, :] <= qpos[:, None]
        logits = jnp.where(mask[None, None], s + bias, -jnp.inf)
        p = jax.nn.softmax(logits, axis=-1)
        return jnp.einsum('bhqk,bkhd->bqhd', p.astype(v.dtype), v)

    out = lax.map(one_block, (qb, cb, jnp.arange(nb)))
    return jnp.transpose(out, (1, 0, 2, 3, 4)).reshape(B, S, H, dh)

def sliding_window_sink_attention(q, k, v, sinks):
    B, S, Hq, dh = q.shape
    W = WINDOW
    nb = S // W
    scale = 1.0 / math.sqrt(dh)
    qb = q.reshape(B, nb, W, SWA_KV_HEADS, SWA_GROUP, dh)

    def banded(t):
        tb = t.reshape(B, nb, W, SWA_KV_HEADS, dh)
        prev = jnp.concatenate([jnp.zeros_like(tb[:, :1]), tb[:, :-1]], axis=1)
        return jnp.concatenate([prev, tb], axis=2)

    kk, vv = banded(k), banded(v)
    s = jnp.einsum('bnqhgd,bnkhd->bnhgqk', qb, kk, preferred_element_type=jnp.float32) * scale
    i = jnp.arange(W)[:, None]
    j = jnp.arange(2 * W)[None, :]
    diff = W + i - j
    key_abs = jnp.arange(nb)[:, None, None] * W + j[None] - W
    mask = (diff >= 0)[None] & (diff < WINDOW)[None] & (key_abs >= 0)
    s = jnp.where(mask[None, :, None, None], s, -jnp.inf)
    sink = sinks.astype(jnp.float32).reshape(SWA_KV_HEADS, SWA_GROUP)[None, None, :, :, None, None]
    m = jnp.maximum(jnp.max(s, axis=-1, keepdims=True), sink)
    e = jnp.exp(s - m)
    denom = jnp.sum(e, axis=-1, keepdims=True) + jnp.exp(sink - m)
    p = e / denom
    out = jnp.einsum('bnhgqk,bnkhd->bnqhgd', p.astype(v.dtype), vv)
    return out.reshape(B, S, Hq, dh)

def hybrid_mixer(x, w_in, b_forget, attn_sinks, w_o_fox, w_o_swa, w_out):
    B, S, _ = x.shape
    proj = jnp.einsum('bsd,dc->bsc', x, w_in)
    sizes = [FOX_W, FOX_W, FOX_W, FOX_HEADS, SWA_QW, SWA_KVW, SWA_KVW, D_MODEL, D_MODEL]
    idx = list(np.cumsum(sizes)[:-1])
    q_f, k_f, v_f, f_logit, q_s, k_s, v_s, g_f, g_s = jnp.split(proj, idx, axis=-1)
    log_f = jax.nn.log_sigmoid((f_logit + b_forget).astype(jnp.float32))
    o_f = forgetting_attention(q_f.reshape(B, S, FOX_HEADS, HEAD_DIM),
                               k_f.reshape(B, S, FOX_HEADS, HEAD_DIM),
                               v_f.reshape(B, S, FOX_HEADS, HEAD_DIM), log_f)
    o_f = jnp.einsum('bsc,cd->bsd', o_f.reshape(B, S, FOX_W), w_o_fox)
    pos = jnp.arange(S, dtype=jnp.float32)
    qs = apply_rope(q_s.reshape(B, S, SWA_Q_HEADS, HEAD_DIM), pos)
    ks = apply_rope(k_s.reshape(B, S, SWA_KV_HEADS, HEAD_DIM), pos)
    o_s = sliding_window_sink_attention(qs, ks, v_s.reshape(B, S, SWA_KV_HEADS, HEAD_DIM), attn_sinks)
    o_s = jnp.einsum('bsc,cd->bsd', o_s.reshape(B, S, SWA_QW), w_o_swa)
    merged = jax.nn.sigmoid(g_f) * o_f + jax.nn.sigmoid(g_s) * o_s
    return jnp.einsum('bsd,de->bse', merged, w_out)

def swiglu_ffn(x, w_gate, w_up, w_down):
    h = jax.nn.silu(jnp.einsum('bsd,df->bsf', x, w_gate)) * jnp.einsum('bsd,df->bsf', x, w_up)
    return jnp.einsum('bsf,fd->bsd', h, w_down)

def setup_inputs(seed: int = 0) -> dict:
    key = jax.random.key(seed)
    ks = jax.random.split(key, 16)
    L = DEPTH
    nrm = jax.random.normal
    x = nrm(ks[0], (BATCH, SEQ, D_MODEL), jnp.float32)
    col_scale = jnp.concatenate([
        jnp.ones((2 * FOX_W,), jnp.float32),
        jnp.full((FOX_W,), DEEPNORM_BETA, jnp.float32),
        jnp.ones((FOX_HEADS + SWA_QW + SWA_KVW,), jnp.float32),
        jnp.full((SWA_KVW,), DEEPNORM_BETA, jnp.float32),
        jnp.ones((2 * D_MODEL,), jnp.float32)])
    w_in = nrm(ks[1], (L, D_MODEL, IN_COLS), jnp.float32) * (D_MODEL ** -0.5) * col_scale
    b_forget = 1.0 + 0.1 * nrm(ks[2], (L, FOX_HEADS), jnp.float32)
    attn_sinks = 0.5 * nrm(ks[3], (L, SWA_Q_HEADS), jnp.float32)
    w_o_fox = nrm(ks[4], (L, FOX_W, D_MODEL), jnp.float32) * (FOX_W ** -0.5)
    w_o_swa = nrm(ks[5], (L, SWA_QW, D_MODEL), jnp.float32) * (SWA_QW ** -0.5)
    w_out = nrm(ks[6], (L, D_MODEL, D_MODEL), jnp.float32) * (D_MODEL ** -0.5) * DEEPNORM_BETA
    ln1_g = 1.0 + 0.02 * nrm(ks[7], (L, D_MODEL), jnp.float32)
    ln1_b = 0.02 * nrm(ks[8], (L, D_MODEL), jnp.float32)
    w_gate = nrm(ks[9], (L, D_MODEL, D_FF), jnp.float32) * (D_MODEL ** -0.5)
    w_up = nrm(ks[10], (L, D_MODEL, D_FF), jnp.float32) * (D_MODEL ** -0.5)
    w_down = nrm(ks[11], (L, D_FF, D_MODEL), jnp.float32) * (D_FF ** -0.5) * DEEPNORM_BETA
    ln2_g = 1.0 + 0.02 * nrm(ks[12], (L, D_MODEL), jnp.float32)
    ln2_b = 0.02 * nrm(ks[13], (L, D_MODEL), jnp.float32)
    return {"x": x, "w_in": w_in, "b_forget": b_forget, "attn_sinks": attn_sinks,
            "w_o_fox": w_o_fox, "w_o_swa": w_o_swa, "w_out": w_out,
            "ln1_g": ln1_g, "ln1_b": ln1_b, "w_gate": w_gate, "w_up": w_up,
            "w_down": w_down, "ln2_g": ln2_g, "ln2_b": ln2_b}

def reference(x, w_in, b_forget, attn_sinks, w_o_fox, w_o_swa, w_out,
              ln1_g, ln1_b, w_gate, w_up, w_down, ln2_g, ln2_b):
    h = x
    for l in range(DEPTH):
        mix = hybrid_mixer(h, w_in[l], b_forget[l], attn_sinks[l], w_o_fox[l], w_o_swa[l], w_out[l])
        h = layer_norm(DEEPNORM_ALPHA * h + mix, ln1_g[l], ln1_b[l])
        ff = swiglu_ffn(h, w_gate[l], w_up[l], w_down[l])
        h = layer_norm(DEEPNORM_ALPHA * h + ff, ln2_g[l], ln2_b[l])
    return h


_drawn_inputs = setup_inputs


def setup_inputs(seed=0):
    import zlib

    import numpy as np

    out = dict(_drawn_inputs(seed))
    spreads = {}
    factors = {'b_forget': 64.0,
     'attn_sinks': 31.676,
     'ln1_g': 2.756,
     'ln1_b': 2.87,
     'ln2_g': 8.362,
     'ln2_b': 7.942}
    for name, (base, spread) in spreads.items():
        noise = np.random.default_rng([zlib.crc32(name.encode()), seed]).standard_normal(out[name].shape)
        drawn = base * np.exp(spread * noise) if base else spread * noise
        out[name] = __import__('jax').numpy.asarray(drawn.astype(out[name].dtype))
    for name, factor in factors.items():
        out[name] = (out[name] * factor).astype(out[name].dtype)
    return out
```

```python
from contextlib import ExitStack

import numpy as np

import concourse.bass as bass
from concourse import mybir

ALU = mybir.AluOpType
ACT = mybir.ActivationFunctionType
F32 = mybir.dt.float32
F32R = mybir.dt.float32r
BF16 = mybir.dt.bfloat16
AX_X = mybir.AxisListType.X

P = 128
SEQ = 512
D = 1024
D_FF = 2816
HD = 64
HEADS = 8
FOX_W = HEADS * HD
KV_W = 2 * HD
ALPHA = 2.0 ** 0.25
LN_EPS = 1e-5
SCALE = 1.0 / HD ** 0.5
NEG = -1.0e30
TB = SEQ // P
KC = D // P
FT = D_FF // P

N_KS = 0
N_QS = (1, 2, 4, 5)
N_VF = 3
N_QF = 6
N_KF = 10
N_V = 14
N_G = 18
N_WO = 34
N_WOUT = 42
N_FF = 50
N_DN = N_FF + 2 * FT
SLABS = N_DN + FT
VF_W = KV_W + HEADS
RAW = 2
SPL = 4
AHEAD = SPL - 1

WOUT_TAIL = 3
DN_TAIL = 4

UNITS = 16
V_BANKS = (2, 3, 4, 7)
WOUT_BANKS = ((6, 7), (0, 1), (2, 3), (4, 5))
DN_BANKS = ((2, 3), (4, 5), (6, 7), (0, 1))
FF_BANKS = ((6, 7), (0, 1))
O_BANK = 1


def unit_step(a):
    return 6 + a if a < 8 else 19 + a - 8


def units_at(n, stage):
    return [a for a in range(UNITS) if unit_step(a) + stage == n]


def proj_bank(n):
    if n < N_V:
        return 0 if n % 2 else 7
    return 1 if n >= 30 and n % 2 == 0 else 0


def score_regions(a):
    if a < 8:
        return [(2, 0, 128, 0, 0), (2, 128, 256, 0, 128), (3, 0, 256, 1, 384), (3, 256, 256, 2, 640)]
    return [(2, 0, 128, 0, 0), (3, 0, 256, 0, 128), (2, 128, 384, 0, 384), (4, 0, 512, 0, 768)]


def key_regions(a):
    if a < 8:
        return [(0, 256), (256, 256), (512, 256), (768, 128)]
    return [(0, 512), (512, 384), (1024, 256), (896, 128)]


def pt_parts(a):
    return [(5, 512), (6, 384)] if a < 8 else [(5, 512), (6, 512), (7, 256)]


def unit_place(a):
    u = a % 8
    return u // 2, u % 2


def program(nc, xT, x, slabs, vf_slab, rope, sel, b_forget, sinks, ln1_g, ln1_b, ln2_g, ln2_b, out):
    ctx = ExitStack()
    with ctx:
        base = -(-nc.sbuf_base // 64) * 64

        def at(name, kb, shape, dt=F32):
            return nc.alloc_sbuf_tensor_at(name, shape, dt, offset=base + int(kb * 1024))

        def sem(name):
            return ctx.enter_context(nc.semaphore(name))

        xh = at("xh", 0, [P, KC, SEQ], F32R)
        xl = at("xl", 16, [P, KC, SEQ], F32R)
        mh = at("mh", 0, [P, KC, SEQ], F32R)
        ml = at("ml", 16, [P, KC, SEQ], F32R)
        ah = at("ah", 0, [P, SPL, SEQ], F32R)
        al = at("al", 8, [P, SPL, SEQ], F32R)
        sg = at("sg", 16, [P, 2, SEQ])
        ln2p = at("ln2p", 20, [P, 2, D])
        x_raw = at("x_raw", 32, [P, KC, SEQ])
        gates = at("gates", 32, [P, KC, 2, SEQ])
        hTh = at("hTh", 32, [P, KC, SEQ], F32R)
        hTl = at("hTl", 48, [P, KC, SEQ], F32R)
        k_f = at("k_f", 64, [P, 4, SEQ])
        v_f = at("v_f", 72, [P, TB, FOX_W])
        res = at("res", 64, [P, TB, D])
        q_f = at("q_f", 80, [P, 4, SEQ])
        q_s = at("q_s", 88, [P, 4, SEQ])
        k_s = at("k_s", 96, [P, SEQ])
        v_s = at("v_s", 98, [P, TB, KV_W])
        prob = at("prob", 100, [P, 1280])
        probT = at("probT", 105, [P, 1280])
        rope1 = at("rope1", 100, [P, SEQ])
        rope2 = at("rope2", 102, [P, SEQ])
        mt1 = at("mt1", 100, [P, SEQ])
        mt2 = at("mt2", 102, [P, SEQ])
        mg = at("mg", 104, [P, 2, SEQ])
        oh = at("oh", 110, [P, 8, SEQ], F32R)
        ol = at("ol", 126, [P, 8, SEQ], F32R)
        ln1p = at("ln1p", 80, [P, 2, D])
        ffT = at("ffT", 80, [P, FT, SEQ])
        raw = at("raw", 142, [P, RAW * D + 64])
        sh = at("sh", 150.25, [P, SPL * D + 64], F32R)
        sl = at("sl", 166.5, [P, SPL * D + 64], F32R)
        cs = at("cs", 182.75, [P, 2, SEQ])
        ident = at("ident", 186.75, [P, P])
        tri = at("tri", 187.25, [P, P])
        ones = at("ones", 187.75, [P, P])
        ident_b = at("ident_b", 188.25, [P, P], BF16)
        mask_b = at("mask_b", 188.5, [P, 2 * P], BF16)
        bias_r = at("bias_r", 189, [32, SEQ], F32R)
        bias_l = at("bias_l", 191, [32, 2, SEQ], F32R)
        bias_l32 = at("bias_l32", 195, [32, SEQ])
        stack = at("stack", 197, [P, TB, 64])
        sel_sb = at("sel_sb", 198, [32, HEADS])
        bf_sb = at("bf_sb", 198.125, [P, HEADS])
        sink_sb = at("sink_sb", 198.25, [P, HEADS])
        fg = at("fg", 198.5, [P, 10, TB * HEADS])
        c_hi = at("c_hi", 199.75, [P, TB * HEADS], F32R)
        nmax = at("nmax", 200, [P, 2, 4])
        smax = at("smax", 200.0625, [P, 2, 4])
        den = at("den", 200.125, [P, 2, 4])
        esink = at("esink", 200.1875, [P, 2, 4])
        rden = at("rden", 200.25, [P, 2, 4])
        stats = at("stats", 200.3125, [P, 2, 12])
        mv = at("mv", 200.4375, [P, 2, 2])
        rstd = at("rstd", 200.46875, [P, 2, 4])

        ps = ctx.enter_context(nc.psum_tensor("ps", [P, 8, 512], F32))

        x_landed = [sem(f"x_landed{c}") for c in range(KC)]
        slab_landed = [sem(f"slab_landed{r}") for r in range(RAW)]
        small_landed = sem("small_landed")
        res_landed = sem("res_landed")
        ln2_landed = sem("ln2_landed")
        consts_made = sem("consts_made")
        x_hi = sem("x_hi")
        x_lo = sem("x_lo")
        hi_ready = sem("hi_ready")
        lo_ready = sem("lo_ready")
        slab_done = sem("slab_done")
        rope_part = sem("rope_part")
        rope_done = sem("rope_done")
        vs_taken = sem("vs_taken")
        qk_taken = sem("qk_taken")
        v_taken = sem("v_taken")
        gate_taken = sem("gate_taken")
        fg_dve = sem("fg_dve")
        fg_act = sem("fg_act")
        cum_done = sem("cum_done")
        stackT_done = sem("stackT_done")
        bias_ready = sem("bias_ready")
        bias_l_ready = sem("bias_l_ready")
        scores_done = sem("scores_done")
        max_part = sem("max_part")
        max_done = sem("max_done")
        exp_done = sem("exp_done")
        den_part = sem("den_part")
        rden_done = sem("rden_done")
        norm_done = sem("norm_done")
        probT_done = sem("probT_done")
        probT_taken = sem("probT_taken")
        pv_done = sem("pv_done")
        o_hi = sem("o_hi")
        o_lo = sem("o_lo")
        gate_sig = sem("gate_sig")
        merge_part = sem("merge_part")
        merge_taken = sem("merge_taken")
        merge_sum = sem("merge_sum")
        merge_hi = sem("merge_hi")
        merge_lo = sem("merge_lo")
        block_done = sem("block_done")
        ln_dve = sem("ln_dve")
        ln_act = sem("ln_act")
        ln_scaled = sem("ln_scaled")
        ln_done = sem("ln_done")
        hT_done = sem("hT_done")
        hT_hi = sem("hT_hi")
        hT_ready = sem("hT_ready")
        silu_done = sem("silu_done")
        ff_free = sem("ff_free")
        a_hi = sem("a_hi")
        a_lo = sem("a_lo")
        out_landed = sem("out_landed")

        def slot(ring, n, width=D):
            s = n % SPL
            return ring[:, s * D:s * D + width]

        def width_of(n):
            return KC * VF_W if n == N_VF else D

        block = ctx.enter_context(nc.Block())

        @block.sync
        def _(sp):
            def load(n):
                if n >= RAW:
                    sp.wait_ge(lo_ready, n - RAW + 1)
                r = n % RAW
                if n == N_VF:
                    src = vf_slab
                else:
                    src = slabs[n - (n > N_VF)]
                sp.dma_start(raw[:, r * D:r * D + width_of(n)], src).then_inc(slab_landed[r], 16)

            sp.dma_start(x_raw[:, 0, :], xT[0]).then_inc(x_landed[0], 16)
            load(0)
            for c in range(1, KC):
                sp.dma_start(x_raw[:, c, :], xT[c]).then_inc(x_landed[c], 16)
            for n in range(1, 6):
                load(n)
            with sp.Fori(0, (SLABS - 6) // RAW) as i:
                for r in range(RAW):
                    sp.wait_ge(lo_ready, i * RAW + (6 + r - RAW + 1))
                    sp.dma_start(raw[:, r * D:(r + 1) * D],
                                 slabs[bass.ds(i * RAW + (5 + r), 1)].rearrange("a p n -> (a p) n"))\
                        .then_inc(slab_landed[r], 16)
            for t in range(TB):
                sp.wait_ge(ln_done, TB + t + 1)
                sp.dma_start(out[t * P:(t + 1) * P, :], res[:, t, :]).then_inc(out_landed, 16)
            sp.wait_ge(out_landed, 16 * TB)

        @block.gpsimd
        def _(pool):
            pool.dma_start(cs[:, :, :], rope).then_inc(small_landed, 16)
            pool.dma_start(sel_sb[:, :], sel).then_inc(small_landed, 16)
            pool.dma_start(bf_sb[:, :], b_forget.partition_broadcast(P)).then_inc(small_landed, 16)
            pool.dma_start(sink_sb[:, :], sinks.partition_broadcast(P)).then_inc(small_landed, 16)
            pool.memset(ident[:, :], 0.0).then_inc(consts_made, 1)
            pool.memset(ones[:, :], 1.0).then_inc(consts_made, 1)
            pool.memset(mask_b[:, :], 0.0).then_inc(consts_made, 1)
            pool.memset(stack[:, :, :], 1.0).then_inc(consts_made, 1)
            pool.wait_ge(consts_made, 4)
            pool.affine_select(out=ident[:, :], in_=ident[:, :], compare_op=ALU.not_equal, fill=1.0,
                               base=0, pattern=[[-1, P]], channel_multiplier=1).then_inc(consts_made, 1)
            pool.affine_select(out=tri[:, :], in_=ones[:, :], compare_op=ALU.is_ge, fill=0.0,
                               base=0, pattern=[[1, P]], channel_multiplier=-1).then_inc(consts_made, 1)
            pool.affine_select(out=mask_b[:, 0:P], in_=mask_b[:, 0:P], compare_op=ALU.is_gt, fill=NEG,
                               base=0, pattern=[[1, P]], channel_multiplier=-1).then_inc(consts_made, 1)
            pool.affine_select(out=mask_b[:, P:2 * P], in_=mask_b[:, P:2 * P], compare_op=ALU.is_ge, fill=NEG,
                               base=0, pattern=[[-1, P]], channel_multiplier=1).then_inc(consts_made, 1)
            pool.wait_ge(consts_made, 8)
            pool.tensor_copy(ident_b[:, :], ident[:, :]).then_inc(consts_made, 1)
            for a in range(UNITS):
                pool.wait_ge(exp_done, a + 1)
                pool.wait_ge(rden_done, a + 1)
                for i, (_, _, w, _, off) in enumerate(score_regions(a)):
                    last = pool.tensor_scalar(prob[:, off:off + w], prob[:, off:off + w],
                                              rden[:, a % 2, i:i + 1], None, ALU.mult)
                last.then_inc(norm_done, 1)
            pool.wait_ge(pv_done, UNITS)
            pool.dma_start(res[:, :, :], x.rearrange("(t p) d -> p t d", p=P)).then_inc(res_landed, 16)
            pool.dma_start(ln1p[:, 0, :], ln1_g.partition_broadcast(P)).then_inc(res_landed, 16)
            pool.dma_start(ln1p[:, 1, :], ln1_b.partition_broadcast(P)).then_inc(res_landed, 16)
            for ln in range(2):
                for t in range(TB):
                    pool.wait_ge(ln_scaled, ln * TB + t + 1)
                    beta = (ln1p, ln2p)[ln][:, 1, :]
                    pool.tensor_tensor(res[:, t, :], res[:, t, :], beta, ALU.add).then_inc(ln_done, 1)
                if ln == 0:
                    pool.wait_ge(slab_done, N_FF)
                    pool.dma_start(ln2p[:, 0, :], ln2_g.partition_broadcast(P)).then_inc(ln2_landed, 16)
                    pool.dma_start(ln2p[:, 1, :], ln2_b.partition_broadcast(P)).then_inc(ln2_landed, 16)

        @block.scalar
        def _(act):
            def slab_hi(n):
                act.wait_ge(slab_landed[n % RAW], 16 * (n // RAW + 1))
                if n >= SPL:
                    act.wait_ge(slab_done, n - SPL + 1)
                r, w = n % RAW, width_of(n)
                act.activation(slot(sh, n, w), raw[:, r * D:r * D + w], ACT.Copy).then_inc(hi_ready, 1)

            def take(n):
                b = proj_bank(n)
                if n == N_VF:
                    act.wait_ge(fg_dve, 1)
                    act.activation(v_s[:, :, :].rearrange("p (a b) c -> p a b c", a=2),
                                   ps[:, 2:4, 0:2 * VF_W].rearrange("p a (b c) -> p a b c", b=2)[:, :, :, 0:KV_W],
                                   ACT.Copy).then_inc(vs_taken, 1)
                elif N_QF <= n < N_KF:
                    act.wait_ge(slab_done, n + 1)
                    act.activation(q_f[:, n - N_QF, :], ps[:, b, :], ACT.Copy, scale=SCALE).then_inc(qk_taken, 1)
                elif N_KF <= n < N_V:
                    act.wait_ge(slab_done, n + 1)
                    act.activation(k_f[:, n - N_KF, :], ps[:, b, :], ACT.Copy).then_inc(qk_taken, 1)
                elif n == N_G - 1:
                    act.wait_ge(slab_done, n + 1)
                    for t in range(TB):
                        act.activation(v_f[:, t, :], ps[:, V_BANKS[t], :], ACT.Copy).then_inc(v_taken, 1)
                elif N_G <= n < N_WO:
                    act.wait_ge(slab_done, n + 1)
                    m, w = (n - N_G) // 2, (n - N_G) % 2
                    act.activation(gates[:, m, w, :], ps[:, b, :], ACT.Copy).then_inc(gate_taken, 1)

            def exps(a):
                b = a % 2
                act.wait_ge(max_done, a + 1)
                if a >= 1:
                    act.wait_ge(probT_done, a)
                if a >= 2:
                    act.wait_ge(norm_done, a - 1)
                if a < 8:
                    j, g = unit_place(a)
                    h = j + 4 * g
                    act.activation(esink[:, b, :], nmax[:, b, :], ACT.Exp, bias=sink_sb[:, h:h + 1])
                for i, (bank, col, w, _, off) in enumerate(score_regions(a)):
                    last = act.activation(prob[:, off:off + w], ps[:, bank, col:col + w], ACT.Exp,
                                          bias=nmax[:, b, i:i + 1], accum_out=den[:, b, i:i + 1])
                last.then_inc(exp_done, 1)

            def take_o(a):
                j, g = unit_place(a)
                rows = slice(g * HD, (g + 1) * HD)
                tile = j + (4 if a < 8 else 0)
                act.wait_ge(pv_done, a + 1)
                act.activation(oh[rows, tile, :], ps[rows, O_BANK, :], ACT.Copy).then_inc(o_hi, 1)

            def rstd_root(k):
                act.wait_ge(ln_dve, 2 * k + 1)
                act.activation(rstd[:, k % 2, 1:2], rstd[:, k % 2, 0:1], ACT.Sqrt).then_inc(ln_act, 1)

            def h_hi(t):
                act.wait_ge(hT_done, t + 1)
                for half in range(2):
                    src = ps[:, WOUT_BANKS[t][half], :].rearrange("p (c q) -> p c q", c=4)
                    act.activation(hTh[:, 4 * half:4 * half + 4, t * P:(t + 1) * P], src, ACT.Copy)\
                        .then_inc(hT_hi, 1)

            for c in range(KC):
                act.wait_ge(x_landed[c], 16)
                act.activation(xh[:, c, :], x_raw[:, c, :], ACT.Copy).then_inc(x_hi, 1)
                if c == 0:
                    slab_hi(0)
            for n in range(1, AHEAD + 1):
                slab_hi(n)
            for n in range(1, N_FF):
                take(n - 1)
                if n == N_VF + 2:
                    act.wait_ge(fg_dve, 3)
                    act.activation(fg[:, 2, :], fg[:, 1, :], ACT.Exp, scale=-1.0).then_inc(fg_act, 1)
                    act.wait_ge(fg_dve, 4)
                    act.activation(fg[:, 4, :], fg[:, 3, :], ACT.Ln).then_inc(fg_act, 1)
                for a in units_at(n, 2):
                    take_o(a)
                for a in units_at(n, 0):
                    exps(a)
                if N_WO <= n < N_WOUT:
                    m = n - N_WO
                    act.wait_ge(gate_taken, 2 * m + 2)
                    act.activation(gates[:, m, :, :], gates[:, m, :, :], ACT.Sigmoid).then_inc(gate_sig, 1)
                if n < N_FF - WOUT_TAIL + 1:
                    slab_hi(n + AHEAD)
                if N_WO < n <= N_WOUT:
                    m = n - 1 - N_WO
                    act.wait_ge(merge_sum, m + 1)
                    act.activation(mh[:, m, :], mg[:, m % 2, :], ACT.Copy).then_inc(merge_hi, 1)
            rstd_root(0)
            rstd_root(1)
            h_hi(0)
            rstd_root(2)
            h_hi(1)
            slab_hi(N_FF + 1)
            slab_hi(N_FF + 2)
            rstd_root(3)
            h_hi(2)
            h_hi(3)

            def a_split_hi(k):
                act.wait_ge(ff_free, k + 3)
                c = k % SPL if isinstance(k, int) else None
                return c

            with act.Fori(0, FT // 2) as i:
                for r in range(4):
                    m = N_FF + r + AHEAD
                    act.wait_ge(slab_landed[m % RAW], i * (16 * 4 // RAW) + 16 * (m // RAW + 1))
                    act.wait_ge(slab_done, i * 4 + (m - SPL + 1))
                    act.activation(slot(sh, m), raw[:, (m % RAW) * D:(m % RAW + 1) * D], ACT.Copy)\
                        .then_inc(hi_ready, 1)
                    if r % 2:
                        fi = r // 2
                        act.wait_ge(slab_done, i * 4 + (N_FF + r))
                        act.wait_ge(ff_free, i * 2 + (fi + 1))
                        act.activation(sg[:, fi, :], ps[:, FF_BANKS[fi][0], :], ACT.Silu).then_inc(silu_done, 1)
            for k in range(2):
                act.activation(ah[:, k, :], ffT[:, k, :], ACT.Copy).then_inc(a_hi, 1)

            def down_step(i, r, slab, split):
                m = N_DN + r + AHEAD
                if slab:
                    act.wait_ge(slab_landed[m % RAW], i * (16 * 4 // RAW) + 16 * (m // RAW + 1))
                    act.wait_ge(slab_done, i * 4 + (m - SPL + 1))
                    act.activation(slot(sh, m), raw[:, (m % RAW) * D:(m % RAW + 1) * D], ACT.Copy)\
                        .then_inc(hi_ready, 1)
                if split:
                    act.wait_ge(slab_done, i * 4 + (N_DN + r + 2 - SPL + 1))
                    act.wait_ge(ff_free, i * 4 + (r + 5))
                    act.activation(ah[:, (r + 2) % SPL, :], ffT[:, bass.ds(i * 4 + (r + 2), 1), :], ACT.Copy)\
                        .then_inc(a_hi, 1)

            with act.Fori(0, 4) as i:
                for r in range(4):
                    down_step(i, r, True, True)
            for r in range(4):
                down_step(4, r, 16 + r + AHEAD < FT, 16 + r + 2 < FT)
            for t in range(TB):
                rstd_root(TB + t)

        @block.vector
        def _(dve):
            def slab_lo(n):
                dve.wait_ge(hi_ready, n + 1)
                r, w = n % RAW, width_of(n)
                dve.tensor_tensor(slot(sl, n, w), raw[:, r * D:r * D + w], slot(sh, n, w).bitcast(F32),
                                  ALU.subtract).then_inc(lo_ready, 1)

            def rope_tile(n, k):
                b = proj_bank(n)
                dst = k_s[:, :] if n == N_KS else q_s[:, N_QS.index(n), :]
                scale = 1.0 if n == N_KS else SCALE
                dve.wait_ge(slab_done, n + 1)
                if k == 0:
                    dve.wait_ge(small_landed, 64)
                else:
                    dve.wait_ge(rope_done, k)
                dve.scalar_tensor_tensor(out=rope1[:, :], in0=ps[:, b, :], scalar=scale, in1=cs[:, 0, :],
                                         op0=ALU.mult, op1=ALU.mult).then_inc(rope_part, 1)
                for q in range(4):
                    src, dst_q = slice(32 * q, 32 * q + 32), slice(32 * (q ^ 1), 32 * (q ^ 1) + 32)
                    dve.scalar_tensor_tensor(out=rope2[dst_q, :], in0=ps[src, b, :], scalar=scale,
                                             in1=cs[src, 1, :], op0=ALU.mult, op1=ALU.mult).then_inc(rope_part, 1)
                dve.wait_ge(rope_part, 5 * (k + 1))
                dve.tensor_tensor(dst, rope1[:, :], rope2[:, :], ALU.add).then_inc(rope_done, 1)

            fgn = [0]

            def fg_step(ins):
                fgn[0] += 1
                ins.then_inc(fg_dve, 1)
                dve.wait_ge(fg_dve, fgn[0])

            def forget_gate_1():
                z, az, e, u, lnu = (fg[:, k, :] for k in range(5))
                dve.wait_ge(slab_done, N_VF + 1)
                logit = ps[:, 2:4, 0:2 * VF_W].rearrange("p a (b c) -> p a b c", b=2)[:, :, :, KV_W:VF_W]
                bf = bf_sb[:, :].unsqueeze(1).unsqueeze(1).broadcast_to([P, 2, 2, HEADS])
                fg_step(dve.tensor_tensor(z.rearrange("p (a b h) -> p a b h", a=2, b=2), logit, bf, ALU.add))
                fg_step(dve.tensor_scalar(az, z, -1.0, None, ALU.mult))
                fg_step(dve.tensor_tensor(az, z, az, ALU.max))

            def forget_gate_2():
                z, az, e, u, lnu, um, d, ru, mn, lf = (fg[:, k, :] for k in range(10))
                dve.wait_ge(fg_act, 1)
                fg_step(dve.tensor_scalar(u, e, 1.0, None, ALU.add))
                fg_step(dve.tensor_scalar(um, u, -1.0, None, ALU.add))
                fg_step(dve.tensor_tensor(d, e, um, ALU.subtract))
                fg_step(dve.reciprocal(ru, u))
                fg_step(dve.tensor_tensor(d, d, ru, ALU.mult))
                fg_step(dve.tensor_scalar(mn, z, 0.0, None, ALU.min))
                fg_step(dve.tensor_tensor(mn, mn, d, ALU.subtract))
                dve.wait_ge(fg_act, 2)
                fg_step(dve.tensor_tensor(lf, mn, lnu, ALU.subtract))

            def bias_stacks():
                dve.wait_ge(cum_done, 1)
                c_sb, c_lo = fg[:, 0, :], fg[:, 1, :]
                fg_step(dve.tensor_copy(c_sb, ps[:, 4, 0:TB * HEADS]))
                fg_step(dve.tensor_copy(c_hi[:, :], c_sb))
                fg_step(dve.tensor_tensor(c_lo, c_sb, c_hi[:, :].bitcast(F32), ALU.subtract))
                dve.wait_ge(consts_made, 4)
                th = lambda ap: ap.rearrange("p (t h) -> p t h", t=TB)
                fg_step(dve.tensor_scalar(stack[:, :, 0:8], th(c_hi[:, :].bitcast(F32)), -1.0, None, ALU.mult))
                fg_step(dve.tensor_scalar(stack[:, :, 8:16], th(c_lo), -1.0, None, ALU.mult))
                fg_step(dve.tensor_copy(stack[:, :, 48:56], th(c_hi[:, :].bitcast(F32))))
                fg_step(dve.tensor_copy(stack[:, :, 56:64], th(c_lo)))

            def take_stacks():
                dve.wait_ge(stackT_done, 1)
                dve.tensor_copy(bias_r[:, :], ps[0:32, 4, :]).then_inc(bias_ready, 1)
                dve.tensor_copy(bias_l32[:, :], ps[32:64, 4, :]).then_inc(bias_ready, 1)

            def head_bias(h):
                dve.wait_ge(bias_ready, 2)
                if h >= 2:
                    dve.wait_ge(scores_done, 8 + h - 1)
                dve.tensor_scalar(bias_l[:, h % 2, :], bias_l32[:, :], sel_sb[:, h:h + 1], None, ALU.mult)\
                    .then_inc(bias_l_ready, 1)

            def maxima(a):
                b = a % 2
                dve.wait_ge(scores_done, a + 1)
                if a >= 2:
                    dve.wait_ge(exp_done, a - 1)
                j, g = unit_place(a)
                for i, (bank, col, w, _, _) in enumerate(score_regions(a)):
                    s = ps[:, bank, col:col + w]
                    if a < 8:
                        dve.tensor_reduce(smax[:, b, i:i + 1], s, AX_X, ALU.max).then_inc(max_part, 1)
                    else:
                        last = dve.tensor_reduce(nmax[:, b, i:i + 1], s, AX_X, ALU.max, negate=True)
                if a < 8:
                    h = j + 4 * g
                    dve.wait_ge(max_part, 4 * (a + 1))
                    last = dve.tensor_scalar(nmax[:, b, :], smax[:, b, :], sink_sb[:, h:h + 1], -1.0,
                                             ALU.max, ALU.mult)
                last.then_inc(max_done, 1)

            def reciprocals(a):
                b = a % 2
                dve.wait_ge(exp_done, a + 1)
                if a < 8:
                    dve.tensor_tensor(den[:, b, :], den[:, b, :], esink[:, b, :], ALU.add).then_inc(den_part, 1)
                    dve.wait_ge(den_part, a + 1)
                dve.reciprocal(rden[:, b, :], den[:, b, :]).then_inc(rden_done, 1)

            def take_probT(a):
                dve.wait_ge(probT_done, a + 1)
                if a >= 1:
                    dve.wait_ge(pv_done, a)
                for k, (bank, w) in enumerate(pt_parts(a)):
                    last = dve.tensor_copy(probT[:, 512 * k:512 * k + w], ps[:, bank, 0:w])
                last.then_inc(probT_taken, 1)

            def take_o(a):
                j, g = unit_place(a)
                rows = slice(g * HD, (g + 1) * HD)
                tile = j + (4 if a < 8 else 0)
                dve.wait_ge(o_hi, a + 1)
                dve.tensor_tensor(ol[rows, tile, :], ps[rows, O_BANK, :], oh[rows, tile, :].bitcast(F32),
                                  ALU.subtract).then_inc(o_lo, 1)

            def merge(m):
                b = 2 + 2 * (m % 2)
                dve.wait_ge(slab_done, N_WO + m + 1)
                dve.wait_ge(gate_sig, m + 1)
                if m >= 1:
                    dve.wait_ge(merge_sum, m)
                dve.tensor_tensor(mt1[:, :], gates[:, m, 0, :], ps[:, b, :], ALU.mult).then_inc(merge_part, 1)
                dve.tensor_tensor(mt2[:, :], gates[:, m, 1, :], ps[:, b + 1, :], ALU.mult).then_inc(merge_taken, 1)
                dve.wait_ge(merge_part, m + 1)
                dve.wait_ge(merge_taken, m + 1)
                if m >= 2:
                    dve.wait_ge(merge_hi, m - 1)
                dve.tensor_tensor(mg[:, m % 2, :], mt1[:, :], mt2[:, :], ALU.add).then_inc(merge_sum, 1)

            def merge_low(m):
                dve.wait_ge(merge_hi, m + 1)
                dve.tensor_tensor(ml[:, m, :], mg[:, m % 2, :], mh[:, m, :].bitcast(F32), ALU.subtract)\
                    .then_inc(merge_lo, 1)

            lnn = [0]

            def ln_step(ins):
                lnn[0] += 1
                ins.then_inc(merge_part, 1)
                dve.wait_ge(merge_part, KC + lnn[0])

            def layer_norm(k):
                ln, t, s = k // TB, k % TB, k % 2
                banks = (WOUT_BANKS, DN_BANKS)[ln][t]
                if k == TB - 1:
                    dve.wait_ge(slab_done, N_FF)
                else:
                    dve.wait_ge(block_done, k + (k < TB))
                if k == 0:
                    dve.wait_ge(res_landed, 48)
                if k == TB:
                    dve.wait_ge(ln2_landed, 32)
                if ln:
                    dve.wait_ge(ln_done, k - TB + 1)
                for half in range(2):
                    r = res[:, t, 512 * half:512 * half + 512]
                    ln_step(dve.scalar_tensor_tensor(out=r, in0=r, scalar=ALPHA, in1=ps[:, banks[half], :],
                                                     op0=ALU.mult, op1=ALU.add))
                    ln_step(dve.bn_stats(stats[:, s, 6 * half:6 * half + 6], r))
                ln_step(dve.bn_aggr(mv[:, s, :], stats[:, s, :]))
                v, root, r0, tmp = (rstd[:, s, q:q + 1] for q in range(4))
                dve.tensor_scalar(v, mv[:, s, 1:2], LN_EPS, None, ALU.add).then_inc(ln_dve, 1)
                dve.wait_ge(ln_act, k + 1)
                ln_step(dve.reciprocal(r0, root))
                ln_step(dve.scalar_tensor_tensor(out=tmp, in0=r0, scalar=v, in1=r0, op0=ALU.mult, op1=ALU.mult))
                ln_step(dve.tensor_scalar(tmp, tmp, -0.5, 1.5, ALU.mult, ALU.add))
                ln_step(dve.tensor_tensor(r0, r0, tmp, ALU.mult))
                r = res[:, t, :]
                dve.tensor_scalar(r, r, mv[:, s, 0:1], r0, ALU.subtract, ALU.mult).then_inc(ln_dve, 1)
                dve.wait_ge(ln_dve, 2 * k + 2)
                gamma = (ln1p, ln2p)[ln][:, 0, :]
                dve.tensor_tensor(r, r, gamma, ALU.mult).then_inc(ln_scaled, 1)

            def h_lo(t):
                for half in range(2):
                    dve.wait_ge(hT_hi, 2 * t + half + 1)
                    src = ps[:, WOUT_BANKS[t][half], :].rearrange("p (c q) -> p c q", c=4)
                    dst = slice(4 * half, 4 * half + 4), slice(t * P, (t + 1) * P)
                    ins = dve.tensor_tensor(hTl[:, dst[0], dst[1]], src, hTh[:, dst[0], dst[1]].bitcast(F32),
                                            ALU.subtract)
                ins.then_inc(ff_free if t < 2 else hT_ready, 1)

            for c in range(KC):
                dve.wait_ge(x_hi, c + 1)
                dve.tensor_tensor(xl[:, c, :], x_raw[:, c, :], xh[:, c, :].bitcast(F32), ALU.subtract)\
                    .then_inc(x_lo, 1)
                if c == 0:
                    slab_lo(0)
            for n in range(1, AHEAD + 1):
                slab_lo(n)
            ropes = [N_KS, *N_QS]
            for n in range(1, N_FF):
                if n - 1 in ropes:
                    rope_tile(n - 1, ropes.index(n - 1))
                if n == N_VF + 1:
                    forget_gate_1()
                if n == N_VF + 2:
                    forget_gate_2()
                for a in units_at(n, 2):
                    take_o(a)
                for a in units_at(n, 1):
                    take_probT(a)
                for a in units_at(n, 0):
                    maxima(a)
                if n == N_QF:
                    bias_stacks()
                if n == N_QF + 1:
                    take_stacks()
                for a in units_at(n + 1, 0):
                    if a >= 8:
                        head_bias(a - 8)
                for a in units_at(n, 0):
                    reciprocals(a)
                if N_WO < n <= N_WOUT:
                    merge(n - 1 - N_WO)
                if n < N_FF - WOUT_TAIL + 1:
                    slab_lo(n + AHEAD)
                if N_WO < n <= N_WOUT:
                    merge_low(n - 1 - N_WO)
            layer_norm(0)
            layer_norm(1)
            h_lo(0)
            layer_norm(2)
            h_lo(1)
            slab_lo(N_FF + 1)
            slab_lo(N_FF + 2)
            layer_norm(3)
            h_lo(2)
            h_lo(3)
            with dve.Fori(0, FT // 2) as i:
                for r in range(4):
                    m = N_FF + r + AHEAD
                    dve.wait_ge(hi_ready, i * 4 + (m + 1))
                    dve.tensor_tensor(slot(sl, m), raw[:, (m % RAW) * D:(m % RAW + 1) * D],
                                      slot(sh, m).bitcast(F32), ALU.subtract).then_inc(lo_ready, 1)
                    if r % 2:
                        fi = r // 2
                        dve.wait_ge(silu_done, i * 2 + (fi + 1))
                        dve.wait_ge(slab_done, i * 4 + (N_FF + r + 1))
                        dve.tensor_tensor(ffT[:, bass.ds(i * 2 + fi, 1), :], sg[:, fi:fi + 1, :],
                                          ps[:, FF_BANKS[fi][1]:FF_BANKS[fi][1] + 1, :], ALU.mult)\
                            .then_inc(ff_free, 1)
            for k in range(2):
                dve.wait_ge(a_hi, k + 1)
                dve.tensor_tensor(al[:, k, :], ffT[:, k, :], ah[:, k, :].bitcast(F32), ALU.subtract)\
                    .then_inc(a_lo, 1)

            def down_step(i, r, slab, split):
                m = N_DN + r + AHEAD
                if slab:
                    dve.wait_ge(hi_ready, i * 4 + (m + 1))
                    dve.tensor_tensor(slot(sl, m), raw[:, (m % RAW) * D:(m % RAW + 1) * D],
                                      slot(sh, m).bitcast(F32), ALU.subtract).then_inc(lo_ready, 1)
                if split:
                    dve.wait_ge(a_hi, i * 4 + (r + 3))
                    s = (r + 2) % SPL
                    dve.tensor_tensor(al[:, s:s + 1, :], ffT[:, bass.ds(i * 4 + (r + 2), 1), :],
                                      ah[:, s:s + 1, :].bitcast(F32), ALU.subtract).then_inc(a_lo, 1)

            with dve.Fori(0, 4) as i:
                for r in range(4):
                    down_step(i, r, True, True)
            for r in range(4):
                down_step(4, r, 16 + r + AHEAD < FT, 16 + r + 2 < FT)
            for t in range(TB):
                layer_norm(TB + t)

        @block.tensor
        def _(pe):
            def mm3(dst, lh, ll, rh, rl, start, stop):
                pe.matmul(dst, lh, rh, start=start, stop=False)
                pe.matmul(dst, ll, rh, start=False, stop=False)
                return pe.matmul(dst, lh, rl, start=False, stop=stop)

            def cut(n, a, b):
                s = (n % SPL) * D
                return sh[:, s + a:s + b], sl[:, s + a:s + b]

            def scores(a):
                j, g = unit_place(a)
                rows = slice(g * HD, (g + 1) * HD)
                regions = score_regions(a)
                if a == 0:
                    pe.wait_ge(vs_taken, 1)
                    pe.wait_ge(fg_dve, 1)
                    pe.wait_ge(consts_made, 9)
                elif a == 8:
                    pe.wait_ge(v_taken, TB)
                    pe.wait_ge(qk_taken, 8)
                else:
                    pe.wait_ge(exp_done, a)
                if a < 8:
                    pe.wait_ge(rope_done, 2 + j)
                else:
                    pe.wait_ge(bias_l_ready, a - 8 + 1)
                seen = set()
                for i, (bank, col, w, k0, _) in enumerate(regions):
                    q = (q_s if a < 8 else q_f)[rows, j, i * P:(i + 1) * P]
                    k = k_s[rows, k0 * P:k0 * P + w] if a < 8 else k_f[rows, j, 0:w]
                    if a < 8:
                        k0 = max(i - 1, 0)
                        k = k_s[rows, k0 * P:k0 * P + w]
                    pe.matmul(ps[:, bank, col:col + w], q, k, start=bank not in seen, stop=False,
                              skip_group_check=True)
                    seen.add(bank)
                if a >= 8:
                    for i, (bank, col, w, _, _) in enumerate(regions):
                        pe.matmul(ps[:, bank, col:col + w], bias_l[:, a % 2, i * P:(i + 1) * P], bias_r[:, 0:w],
                                  start=False, stop=False, skip_group_check=True)
                for i, (bank, col, w, _, _) in enumerate(regions):
                    mw = min(w, 2 * P) if a < 8 else P
                    last = pe.matmul(ps[:, bank, col + w - mw:col + w], ident_b[:, :], mask_b[:, 2 * P - mw:2 * P],
                                     start=False, stop=True, skip_group_check=True)
                last.then_inc(scores_done, 1)

            def transposes(a):
                pe.wait_ge(norm_done, a + 1)
                if a >= 1:
                    pe.wait_ge(probT_taken, a)
                keys = key_regions(a)
                for i, (_, _, w, _, off) in enumerate(score_regions(a)):
                    k0 = i + 1 - w // P
                    for kb in range(k0, i + 1):
                        col = keys[kb][0] + (i - kb) * P
                        last = pe.transpose(ps[:, 5 + col // 512, col % 512:col % 512 + P],
                                            prob[:, off + (kb - k0) * P:off + (kb - k0 + 1) * P], ident[:, :])
                last.then_inc(probT_done, 1)

            def values(a):
                j, g = unit_place(a)
                rows = slice(g * HD, (g + 1) * HD)
                pe.wait_ge(probT_taken, a + 1)
                if a >= 1:
                    pe.wait_ge(o_lo, a)
                for kb, (col, w) in enumerate(key_regions(a)):
                    v = v_s[:, kb, g * HD:(g + 1) * HD] if a < 8 else v_f[:, kb, (a - 8) * HD:(a - 7) * HD]
                    last = pe.matmul(ps[rows, O_BANK, kb * P:kb * P + w], v, probT[:, col:col + w],
                                     start=(kb == 0), stop=(kb == TB - 1), skip_group_check=True)
                last.then_inc(pv_done, 1)

            def cumulative():
                pe.wait_ge(fg_dve, 11)
                pe.wait_ge(consts_made, 9)
                lf = fg[:, 9, :]
                for t in range(TB):
                    dst = ps[:, 4, t * HEADS:(t + 1) * HEADS]
                    for s in range(t):
                        pe.matmul(dst, ones[:, :], lf[:, s * HEADS:(s + 1) * HEADS], start=(s == 0), stop=False)
                    last = pe.matmul(dst, tri[:, :], lf[:, t * HEADS:(t + 1) * HEADS], start=(t == 0), stop=True)
                last.then_inc(cum_done, 1)

            def stacks():
                pe.wait_ge(fg_dve, 18)
                for t in range(TB):
                    last = pe.transpose(ps[0:64, 4, t * P:(t + 1) * P], stack[:, t, :], ident[:, :])
                last.then_inc(stackT_done, 1)

            def bank_free(n):
                if n in (2, 4, 5, 6, 7):
                    pe.wait_ge(rope_done, {2: 1, 4: 3, 5: 2, 6: 4, 7: 5}[n])
                elif 8 <= n < N_V:
                    pe.wait_ge(qk_taken, n - 7)
                elif n == N_V:
                    pe.wait_ge(exp_done, 8)
                    pe.wait_ge(bias_ready, 2)
                    pe.wait_ge(qk_taken, 7)
                elif n == N_G:
                    pe.wait_ge(qk_taken, 8)
                elif N_G < n < 30:
                    pe.wait_ge(gate_taken, n - N_G)
                elif n == 30:
                    pe.wait_ge(o_lo, UNITS)
                elif n < N_WO and n > 30:
                    pe.wait_ge(gate_taken, n - N_G - 1)
                elif n in (N_WO, N_WO + 1):
                    pe.wait_ge(exp_done, UNITS)
                    pe.wait_ge(probT_taken, UNITS)
                elif N_WO + 2 <= n < N_WOUT:
                    pe.wait_ge(merge_taken, n - N_WO - 1)

            def slab(n):
                pe.wait_ge(lo_ready, n + 1)
                bank_free(n)
                b = proj_bank(n)
                if n == N_VF:
                    for t in range(TB):
                        dst = ps[:, 2 + t // 2, (t % 2) * VF_W:(t % 2 + 1) * VF_W]
                        for c in range(KC):
                            tok = slice(t * P, (t + 1) * P)
                            last = mm3(dst, xh[:, c, tok], xl[:, c, tok], *cut(n, c * VF_W, (c + 1) * VF_W),
                                       start=(c == 0), stop=(c == KC - 1))
                elif N_V <= n < N_G:
                    for t in range(TB):
                        for i in range(2):
                            c = 2 * (n - N_V) + i
                            tok = slice(t * P, (t + 1) * P)
                            last = mm3(ps[:, V_BANKS[t], :], xh[:, c, tok], xl[:, c, tok],
                                       *cut(n, i * FOX_W, (i + 1) * FOX_W), start=(c == 0), stop=(c == KC - 1))
                elif n < N_WO:
                    for c in range(KC):
                        if n == 0:
                            pe.wait_ge(x_lo, c + 1)
                        last = mm3(ps[:, b, :], *cut(n, c * P, (c + 1) * P), xh[:, c, :], xl[:, c, :],
                                   start=(c == 0), stop=(c == KC - 1))
                else:
                    pe.wait_ge(o_lo, UNITS)
                    b = 2 + 2 * (n % 2)
                    for c in range(8):
                        last = mm3(ps[:, b + c // 4, :], *cut(n, c * P, (c + 1) * P), oh[:, c, :], ol[:, c, :],
                                   start=(c % 4 == 0), stop=(c % 4 == 3))
                last.then_inc(slab_done, 1)

            def rows_by_block(slabs_, lhs, banks, first, last_c, t):
                for n, c in slabs_:
                    for half in range(2):
                        lh, ll = lhs(c, t)
                        last = mm3(ps[:, banks[t][half], :], lh, ll, *cut(n, 512 * half, 512 * half + 512),
                                   start=(c == first), stop=(c == last_c))
                    yield last

            def merged(c, t):
                return mh[:, c, t * P:(t + 1) * P], ml[:, c, t * P:(t + 1) * P]

            for n in range(N_WOUT):
                for a in units_at(n, 2):
                    values(a)
                for a in units_at(n, 1):
                    transposes(a)
                for a in units_at(n, 0):
                    scores(a)
                if n == N_QF:
                    cumulative()
                if n == N_QF + 1:
                    stacks()
                slab(n)
            for c in range(KC - WOUT_TAIL):
                n = N_WOUT + c
                pe.wait_ge(lo_ready, n + 1)
                pe.wait_ge(merge_lo, c + 1)
                for t in range(TB):
                    if c == 0 and t == 1:
                        pe.wait_ge(gate_taken, 16)
                    if c == 0 and t >= 2:
                        pe.wait_ge(merge_taken, 5 + t)
                    for last in rows_by_block([(n, c)], merged, WOUT_BANKS, 0, KC - 1, t):
                        pass
                last.then_inc(slab_done, 1)

            def turn_h(t):
                pe.wait_ge(ln_done, t + 1)
                for c in range(KC):
                    last = pe.transpose(ps[:, WOUT_BANKS[t][c // 4], (c % 4) * P:(c % 4 + 1) * P],
                                        res[:, t, c * P:(c + 1) * P], ident[:, :])
                last.then_inc(hT_done, 1)

            tail = [(N_WOUT + c, c) for c in range(KC - WOUT_TAIL, KC)]
            for t in range(TB):
                if t == 0:
                    pe.wait_ge(lo_ready, N_FF)
                    pe.wait_ge(merge_lo, KC)
                for k, last in enumerate(rows_by_block(tail, merged, WOUT_BANKS, 0, KC - 1, t)):
                    if t == TB - 1:
                        last.then_inc(slab_done, 1)
                    elif k == len(tail) - 1:
                        last.then_inc(block_done, 1)
                if t == 2:
                    turn_h(0)
            turn_h(1)
            turn_h(2)
            turn_h(3)
            pe.wait_ge(hT_ready, 2)
            with pe.Fori(0, FT // 2) as i:
                for r in range(4):
                    n = N_FF + r
                    pe.wait_ge(lo_ready, i * 4 + (n + 1))
                    if r % 2 == 0:
                        pe.wait_ge(ff_free, i * 2 + (r // 2 + 1))
                    for c in range(KC):
                        last = mm3(ps[:, FF_BANKS[r // 2][r % 2], :], *cut(n, c * P, (c + 1) * P),
                                   hTh[:, c, :], hTl[:, c, :], start=(c == 0), stop=(c == KC - 1))
                    last.then_inc(slab_done, 1)

            def hidden(c, t):
                s = c % SPL
                return ah[:, s, t * P:(t + 1) * P], al[:, s, t * P:(t + 1) * P]

            def down(i, r, peel):
                n = N_DN + r
                pe.wait_ge(lo_ready, i * 4 + (n + 1))
                pe.wait_ge(a_lo, i * 4 + (r + 1))
                for t in range(TB):
                    if peel and t >= 2:
                        pe.wait_ge(ff_free, FT + t - 1)
                    for half in range(2):
                        lh, ll = hidden(r, t)
                        last = mm3(ps[:, DN_BANKS[t][half], :], lh, ll, *cut(n, 512 * half, 512 * half + 512),
                                   start=peel, stop=False)
                last.then_inc(slab_done, 1)

            for r in range(4):
                down(0, r, r == 0)
            with pe.Fori(1, 4) as i:
                for r in range(4):
                    down(i, r, False)
            for r in range(FT - DN_TAIL - 16):
                down(4, r, False)
            tail = [(N_DN + k, k) for k in range(FT - DN_TAIL, FT)]
            for t in range(TB):
                if t == 0:
                    pe.wait_ge(lo_ready, SLABS)
                    pe.wait_ge(a_lo, FT)
                for last in rows_by_block(tail, hidden, DN_BANKS, 0, FT - 1, t):
                    pass
                last.then_inc(block_done, 1)


def rope_table():
    half = HD // 2
    freq = (np.float32(10000.0) ** (-np.arange(half, dtype=np.float32) / np.float32(half))).astype(np.float32)
    ang = (np.arange(SEQ, dtype=np.float32)[None, :] * freq[:, None]).astype(np.float32)
    cos, sin = np.cos(ang).astype(np.float32), np.sin(ang).astype(np.float32)
    return np.ascontiguousarray(np.stack([np.concatenate([cos] * 4), np.concatenate([sin, -sin] * 2)], axis=1))


def head_selector():
    return (np.arange(32)[:, None] % HEADS == np.arange(HEADS)[None, :]).astype(np.float32)


def lay_out_slabs(w_in, w_o_fox, w_o_swa, w_out, w_gate, w_up, w_down):
    cols = np.cumsum([FOX_W, FOX_W, FOX_W, HEADS, FOX_W, KV_W, KV_W, D, D])
    qf, kf, vf, fl, qs, ks, vs, gf, gs = np.split(w_in, cols[:-1], axis=1)

    def by_columns(w):
        n = w.shape[1] // P
        return w.reshape(KC, P, n, P).transpose(2, 1, 0, 3).reshape(n, P, D)

    qs = qs.reshape(D, 2, 4, HD).transpose(0, 2, 1, 3).reshape(D, FOX_W)
    os_ = w_o_swa.reshape(2, 4, HD, D).transpose(1, 0, 2, 3).reshape(FOX_W, D)
    qs, ks = by_columns(qs), by_columns(ks)
    v = vf.reshape(4, 2, P, FOX_W).transpose(0, 2, 1, 3).reshape(4, P, D)
    gates = np.stack([by_columns(gf), by_columns(gs)], axis=1).reshape(16, P, D)
    wo = by_columns(np.concatenate([w_o_fox, os_]))
    ff = np.stack([by_columns(w_gate), by_columns(w_up)], axis=1).reshape(2 * FT, P, D)
    slabs = np.concatenate([ks, qs[:2], qs[2:], by_columns(qf), by_columns(kf), v, gates, wo,
                            w_out.reshape(KC, P, D), ff, w_down.reshape(FT, P, D)])
    vs_f = np.concatenate([vs, fl], axis=1).reshape(KC, P, VF_W).transpose(1, 0, 2).reshape(P, KC * VF_W)
    return np.ascontiguousarray(slabs), np.ascontiguousarray(vs_f)


def kernel(**inputs):
    import concourse.bacc as bacc
    from concourse.bass_utils import run_bass_kernel_spmd

    a = {k: np.asarray(v) for k, v in inputs.items()}
    slabs, vf = lay_out_slabs(*(a[k][0] for k in ("w_in", "w_o_fox", "w_o_swa", "w_out", "w_gate", "w_up", "w_down")))
    arrays = {
        "xT": np.ascontiguousarray(a["x"][0].T.reshape(KC, P, SEQ)),
        "x": np.ascontiguousarray(a["x"][0]),
        "slabs": slabs,
        "vf_slab": vf,
        "rope": rope_table(),
        "sel": head_selector(),
        "b_forget": np.ascontiguousarray(a["b_forget"][0]),
        "sinks": np.ascontiguousarray(a["attn_sinks"][0]),
        "ln1_g": np.ascontiguousarray(a["ln1_g"][0]),
        "ln1_b": np.ascontiguousarray(a["ln1_b"][0]),
        "ln2_g": np.ascontiguousarray(a["ln2_g"][0]),
        "ln2_b": np.ascontiguousarray(a["ln2_b"][0]),
    }
    nc = bacc.Bacc("TRN2", target_bir_lowering=False, num_devices=1)
    args = [nc.dram_tensor(f"in_{k}", v.shape, mybir.dt.from_np(v.dtype), kind="ExternalInput").ap()
            for k, v in arrays.items()]
    out = nc.dram_tensor("out_0", (SEQ, D), F32, kind="ExternalOutput").ap()
    program(nc, *args, out)
    r = run_bass_kernel_spmd(nc, [{f"in_{k}": v for k, v in arrays.items()}], core_ids=[0])
    return r.results[0]["out_0"].reshape(1, SEQ, D)
```

```python
from contextlib import ExitStack

import numpy as np

import concourse.bass as bass
from concourse import mybir

ALU = mybir.AluOpType
ACT = mybir.ActivationFunctionType
F32 = mybir.dt.float32
F32R = mybir.dt.float32r
BF16 = mybir.dt.bfloat16
AX_X = mybir.AxisListType.X

P = 128
SEQ = 512
D = 1024
D_FF = 2816
HD = 64
HEADS = 8
FOX_W = HEADS * HD
KV_W = 2 * HD
ALPHA = 2.0 ** 0.25
LN_EPS = 1e-5
SCALE = 1.0 / HD ** 0.5
NEG = -1.0e30
TB = SEQ // P
KC = D // P
FT = D_FF // P

N_KS = 0
N_QS = (1, 2, 4, 5)
N_VF = 3
N_QF = 6
N_KF = 10
N_V = 14
N_G = 18
N_WO = 34
N_WOUT = 42
N_FF = 50
N_DN = N_FF + 2 * FT
SLABS = N_DN + FT
VF_W = KV_W + HEADS
FIRST = 4
RAW = 2
SPL = 4
AHEAD = SPL - 1

WOUT_TAIL = 4
DN_TAIL = 4

ROPE_SLABS = (N_KS, *N_QS)
POOL_LO = (N_FF + 2, N_FF + 3)
UNITS = 16
V_BANKS = (2, 3, 4, 7)
WOUT_BANKS = ((6, 7), (0, 1), (2, 3), (4, 5))
DN_BANKS = ((2, 3), (4, 5), (6, 7), (0, 1))
FF_BANKS = ((6, 7), (0, 1))
O_BANK = 1


def unit_step(a):
    return 6 + a if a < 8 else 19 + a - 8


def units_at(n, stage):
    return [a for a in range(UNITS) if unit_step(a) + stage == n]


def proj_bank(n):
    if n < N_V:
        return 0 if n % 2 else 7
    return 1 if n >= 30 and n % 2 == 0 else 0


def score_regions(a):
    if a < 8:
        return [(2, 0, 128, 0, 0), (2, 128, 256, 0, 128), (3, 0, 256, 1, 384), (3, 256, 256, 2, 640)]
    return [(2, 0, 128, 0, 0), (3, 0, 256, 0, 128), (2, 128, 384, 0, 384), (4, 0, 512, 0, 768)]


def key_regions(a):
    if a < 8:
        return [(0, 256), (256, 256), (512, 256), (768, 128)]
    return [(0, 512), (512, 384), (1024, 256), (896, 128)]


def pt_parts(a):
    return [(5, 512), (6, 384)] if a < 8 else [(5, 512), (6, 512), (7, 256)]


def probT_parts_before(a):
    return sum(len(pt_parts(b)) for b in range(a))


def half(g):
    return slice(g * HD, (g + 1) * HD)


def unit_place(a):
    u = a % 8
    return u // 2, u % 2


def program(nc, xT, x, slabs, vf_slab, rope, sel, b_forget, sinks, ln1_g, ln1_b, ln2_g, ln2_b, out):
    ctx = ExitStack()
    with ctx:
        base = -(-nc.sbuf_base // 64) * 64

        def at(name, kb, shape, dt=F32):
            return nc.alloc_sbuf_tensor_at(name, shape, dt, offset=base + int(kb * 1024))

        def sem(name):
            return ctx.enter_context(nc.semaphore(name))

        xh = at("xh", 0, [P, KC, SEQ], F32R)
        xl = at("xl", 16, [P, KC, SEQ], F32R)
        mh = at("mh", 0, [P, KC, SEQ], F32R)
        ml = at("ml", 16, [P, KC, SEQ], F32R)
        ah = at("ah", 0, [P, SPL, SEQ], F32R)
        al = at("al", 8, [P, SPL, SEQ], F32R)
        sg = at("sg", 16, [P, 2, SEQ])
        ln2p = at("ln2p", 20, [P, 2, D])
        x_raw = at("x_raw", 32, [P, KC, SEQ])
        q_s = at("q_s", 32, [P, HEADS, SEQ], F32R)
        kh_s = at("kh_s", 48, [P, 2, SEQ], F32R)
        kl_s = at("kl_s", 52, [P, SEQ], F32R)
        v_s = at("v_s", 54, [P, TB, 2, 2 * HD], F32R)
        rope1 = at("rope1", 58, [P, SEQ])
        rope2 = at("rope2", 60, [P, SEQ])
        rope3 = at("rope3", 62, [P, SEQ])
        gates = at("gates", 32, [P, KC, 2, SEQ])
        hTh = at("hTh", 32, [P, KC, SEQ], F32R)
        hTl = at("hTl", 48, [P, KC, SEQ], F32R)
        kh_f = at("kh_f", 64, [P, HEADS, SEQ], F32R)
        kl_f = at("kl_f", 80, [P, 4, SEQ], F32R)
        q_f = at("q_f", 88, [P, HEADS, SEQ], F32R)
        v_f = at("v_f", 104, [P, TB, HEADS, 2 * HD], F32R)
        o_f = at("o_f", 88, [P, 4, 2, SEQ], F32R)
        o_s = at("o_s", 120, [P, 4, 2, SEQ], F32R)
        res = at("res", 64, [P, TB, D])
        ln1p = at("ln1p", 80, [P, 2, D])
        ffT = at("ffT", 88, [P, FT, SEQ])
        first_raw = at("first_raw", 104, [P, FIRST, KC * VF_W])
        tri = at("tri", 132, [P, P])
        ones = at("ones", 132.5, [P, P])
        stack = at("stack", 133, [P, TB, 64])
        prob = at("prob", 136, [P, 1280])
        pth = at("pth", 141, [P, 1280], F32R)
        ptl = at("ptl", 146, [P, 1280], F32R)
        mt1 = at("mt1", 136, [P, SEQ])
        mt2 = at("mt2", 138, [P, SEQ])
        mg = at("mg", 140, [P, 2, SEQ])
        raw = at("raw", 151, [P, RAW * D])
        sh = at("sh", 159, [P, SPL * D + 64], F32R)
        sl = at("sl", 175.25, [P, SPL * D + 64], F32R)
        cs = at("cs", 191.5, [P, 2, SEQ])
        bias_r = at("bias_r", 191.5, [32, SEQ], F32R)
        bias_l32 = at("bias_l32", 193.5, [32, SEQ])
        bias_l = at("bias_l", 195.5, [32, 2, SEQ], F32R)
        ident = at("ident", 199.5, [P, P])
        ident_b = at("ident_b", 200, [P, P], BF16)
        mask_b = at("mask_b", 200.25, [P, 2 * P], BF16)
        o_low = at("o_low", 200.75, [P, SEQ])
        o_sum = at("o_sum", 202.75, [P, SEQ])
        sel_sb = at("sel_sb", 204.75, [32, HEADS])
        bf_sb = at("bf_sb", 204.8125, [P, HEADS])
        sink_sb = at("sink_sb", 204.875, [P, HEADS])
        fg = at("fg", 205, [P, 10, TB * HEADS])
        c_hi = at("c_hi", 206.25, [P, TB * HEADS], F32R)
        nmax = at("nmax", 206.375, [P, 2, 4])
        smax = at("smax", 206.4375, [P, 2, 4])
        den = at("den", 206.5, [P, 2, 4])
        esink = at("esink", 206.5625, [P, 2, 4])
        rden = at("rden", 206.625, [P, 2, 4])
        stats = at("stats", 206.6875, [P, 2, 12])
        mv = at("mv", 206.8125, [P, 2, 2])
        rstd = at("rstd", 206.84375, [P, 2, 4])

        ps = ctx.enter_context(nc.psum_tensor("ps", [P, 8, 512], F32))

        x_landed = [sem(f"x_landed{c}") for c in range(KC)]
        first_landed = [sem(f"first_landed{n}") for n in range(FIRST)]
        slab_landed = [sem(f"slab_landed{r}") for r in range(RAW)]
        small_landed = sem("small_landed")
        res_landed = sem("res_landed")
        ln2_landed = sem("ln2_landed")
        consts_made = sem("consts_made")
        x_hi = sem("x_hi")
        x_lo = sem("x_lo")
        hi_ready = sem("hi_ready")
        lo_ready = sem("lo_ready")
        slab_done = sem("slab_done")
        rope_rot = sem("rope_rot")
        rope_cos = sem("rope_cos")
        rope_sin = sem("rope_sin")
        rope_sum = sem("rope_sum")
        rope_hi = sem("rope_hi")
        rope_done = sem("rope_done")
        vs_taken = sem("vs_taken")
        qk_hi = sem("qk_hi")
        qk_taken = sem("qk_taken")
        v_hi = sem("v_hi")
        v_taken = sem("v_taken")
        gate_taken = sem("gate_taken")
        fg_dve = sem("fg_dve")
        fg_act = sem("fg_act")
        cum_done = sem("cum_done")
        stackT_done = sem("stackT_done")
        bias_ready = sem("bias_ready")
        bias_l_ready = sem("bias_l_ready")
        scores_done = sem("scores_done")
        max_part = sem("max_part")
        max_done = sem("max_done")
        exp_done = sem("exp_done")
        den_part = sem("den_part")
        rden_done = sem("rden_done")
        norm_done = sem("norm_done")
        probT_done = sem("probT_done")
        probT_hi = sem("probT_hi")
        probT_taken = sem("probT_taken")
        pv_done = sem("pv_done")
        o_low_done = sem("o_low_done")
        o_sum_done = sem("o_sum_done")
        o_hi = sem("o_hi")
        o_lo = sem("o_lo")
        gate_sig = sem("gate_sig")
        merge_part = sem("merge_part")
        merge_taken = sem("merge_taken")
        merge_sum = sem("merge_sum")
        merge_hi = sem("merge_hi")
        merge_lo = sem("merge_lo")
        block_done = sem("block_done")
        ln_dve = sem("ln_dve")
        ln_act = sem("ln_act")
        ln_part = sem("ln_part")
        ln_done = sem("ln_done")
        hT_done = sem("hT_done")
        hT_hi = sem("hT_hi")
        hT_ready = sem("hT_ready")
        silu_done = sem("silu_done")
        ff_done = sem("ff_done")
        a_hi = sem("a_hi")
        a_lo = sem("a_lo")
        out_landed = sem("out_landed")

        def slot(ring, n, width=D):
            s = n % SPL
            return ring[:, s * D:s * D + width]

        def raw_of(n):
            if n < FIRST:
                return first_raw[:, n, 0:width_of(n)]
            return raw[:, (n % RAW) * D:(n % RAW + 1) * D]

        def landed_count(n):
            return 16 * ((n - FIRST) // RAW + 1)

        def width_of(n):
            return KC * VF_W if n == N_VF else D

        block = ctx.enter_context(nc.Block())

        @block.sync
        def _(sp):
            def load(n):
                if n < FIRST:
                    src = vf_slab if n == N_VF else slabs[n]
                    sp.dma_start(first_raw[:, n, 0:width_of(n)], src).then_inc(first_landed[n], 16)
                else:
                    sp.dma_start(raw[:, (n % RAW) * D:(n % RAW + 1) * D], slabs[n - 1])\
                        .then_inc(slab_landed[n % RAW], 16)

            sp.dma_start(x_raw[:, 0, :], xT[0]).then_inc(x_landed[0], 16)
            load(0)
            for c in range(1, KC):
                sp.dma_start(x_raw[:, c, :], xT[c]).then_inc(x_landed[c], 16)
            for n in range(1, FIRST + RAW):
                load(n)
            with sp.Fori(0, (SLABS - FIRST - RAW) // RAW) as i:
                for r in range(RAW):
                    n = FIRST + RAW + r
                    sp.wait_ge(lo_ready, i * RAW + (n - RAW + 1))
                    sp.dma_start(raw[:, (n % RAW) * D:(n % RAW + 1) * D],
                                 slabs[bass.ds(i * RAW + (n - 1), 1)].rearrange("a p n -> (a p) n"))\
                        .then_inc(slab_landed[n % RAW], 16)
            for t in range(TB):
                for half in range(2):
                    sp.wait_ge(ln_done, TB + 2 * t + half + 1)
                    cols = slice(512 * half, 512 * half + 512)
                    sp.dma_start(out[t * P:(t + 1) * P, cols], res[:, t, cols]).then_inc(out_landed, 16)
            sp.wait_ge(out_landed, 16 * 2 * TB)

        @block.gpsimd
        def _(pool):
            pool.dma_start(cs[:, :, :], rope).then_inc(small_landed, 16)
            pool.dma_start(sel_sb[:, :], sel).then_inc(small_landed, 16)
            pool.dma_start(bf_sb[:, :], b_forget.partition_broadcast(P)).then_inc(small_landed, 16)
            pool.dma_start(sink_sb[:, :], sinks.partition_broadcast(P)).then_inc(small_landed, 16)
            pool.memset(ident[:, :], 0.0).then_inc(consts_made, 1)
            pool.memset(ones[:, :], 1.0).then_inc(consts_made, 1)
            pool.memset(mask_b[:, :], 0.0).then_inc(consts_made, 1)
            pool.memset(stack[:, :, :], 1.0).then_inc(consts_made, 1)
            pool.wait_ge(consts_made, 4)
            pool.affine_select(out=ident[:, :], in_=ident[:, :], compare_op=ALU.not_equal, fill=1.0,
                               base=0, pattern=[[-1, P]], channel_multiplier=1).then_inc(consts_made, 1)
            pool.affine_select(out=tri[:, :], in_=ones[:, :], compare_op=ALU.is_ge, fill=0.0,
                               base=0, pattern=[[1, P]], channel_multiplier=-1).then_inc(consts_made, 1)
            pool.affine_select(out=mask_b[:, 0:P], in_=mask_b[:, 0:P], compare_op=ALU.is_gt, fill=NEG,
                               base=0, pattern=[[1, P]], channel_multiplier=-1).then_inc(consts_made, 1)
            pool.affine_select(out=mask_b[:, P:2 * P], in_=mask_b[:, P:2 * P], compare_op=ALU.is_ge, fill=NEG,
                               base=0, pattern=[[-1, P]], channel_multiplier=1).then_inc(consts_made, 1)
            pool.wait_ge(consts_made, 8)
            pool.tensor_copy(ident_b[:, :], ident[:, :]).then_inc(consts_made, 1)
            for k in range(len(ROPE_SLABS)):
                pool.wait_ge(rope_rot, k + 1)
                if k == 0:
                    pool.wait_ge(small_landed, 64)
                pool.tensor_tensor(rope3[:, :], rope2[:, :], cs[:, 1, :], ALU.mult).then_inc(rope_sin, 1)
            pool.wait_ge(pv_done, UNITS)
            pool.dma_start(res[:, :, :], x.rearrange("(t p) d -> p t d", p=P)).then_inc(res_landed, 16)
            pool.dma_start(ln1p[:, 0, :], ln1_g.partition_broadcast(P)).then_inc(res_landed, 16)
            pool.dma_start(ln1p[:, 1, :], ln1_b.partition_broadcast(P)).then_inc(res_landed, 16)
            for n in POOL_LO:
                pool.wait_ge(hi_ready, n + 1)
                pool.wait_ge(lo_ready, n)
                pool.tensor_tensor(slot(sl, n), raw_of(n), slot(sh, n).bitcast(F32), ALU.subtract)\
                    .then_inc(lo_ready, 1)
            pool.wait_ge(slab_done, N_FF)
            pool.dma_start(ln2p[:, 0, :], ln2_g.partition_broadcast(P)).then_inc(ln2_landed, 16)
            pool.dma_start(ln2p[:, 1, :], ln2_b.partition_broadcast(P)).then_inc(ln2_landed, 16)

        @block.scalar
        def _(act):
            def slab_hi(n):
                if n < FIRST:
                    act.wait_ge(first_landed[n], 16)
                else:
                    act.wait_ge(slab_landed[n % RAW], landed_count(n))
                    act.wait_ge(slab_done, n - SPL + 1)
                act.activation(slot(sh, n, width_of(n)), raw_of(n), ACT.Copy).then_inc(hi_ready, 1)

            def rope_rotate(n, k):
                b = proj_bank(n)
                act.wait_ge(slab_done, n + 1)
                act.wait_ge(rope_cos, k + 1)
                if k:
                    act.wait_ge(rope_sin, k)
                else:
                    act.wait_ge(x_lo, KC)
                for q in range(4):
                    last = act.activation(rope2[32 * (q ^ 1):32 * (q ^ 1) + 32, :], ps[32 * q:32 * q + 32, b, :],
                                          ACT.Copy, scale=1.0 if n == N_KS else SCALE)
                last.then_inc(rope_rot, 1)

            def rope_split(n, k):
                act.wait_ge(rope_sum, k + 1)
                if n == N_KS:
                    for g in range(2):
                        for dst in range(2):
                            last = act.activation(kh_s[half(dst), g, :], rope1[half(g), :], ACT.Copy)
                else:
                    j = N_QS.index(n)
                    for g in range(2):
                        last = act.activation(q_s[half(g), 2 * j + g, :], rope1[half(g), :], ACT.Copy)
                last.then_inc(rope_hi, 1)

            def take(n):
                b = proj_bank(n)
                if n == N_VF:
                    act.wait_ge(slab_done, n + 1)
                    act.wait_ge(fg_dve, 1)
                    for a in range(2):
                        last = act.activation(
                            v_s[:, 2 * a:2 * a + 2, :, 0:HD],
                            ps[:, 2 + a, 0:2 * VF_W].rearrange("p (b c) -> p b c", b=2)[:, :, 0:KV_W]
                            .rearrange("p b (g d) -> p b g d", g=2), ACT.Copy)
                    last.then_inc(v_hi, 1)
                elif N_QF <= n < N_KF:
                    act.wait_ge(slab_done, n + 1)
                    for g in range(2):
                        last = act.activation(q_f[half(g), 2 * (n - N_QF) + g, :], ps[half(g), b, :], ACT.Copy,
                                              scale=SCALE)
                    last.then_inc(qk_hi, 1)
                elif N_KF <= n < N_V:
                    act.wait_ge(slab_done, n + 1)
                    for g in range(2):
                        for dst in range(2):
                            last = act.activation(kh_f[half(dst), 2 * (n - N_KF) + g, :], ps[half(g), b, :], ACT.Copy)
                    last.then_inc(qk_hi, 1)
                elif n == N_G - 1:
                    act.wait_ge(slab_done, n + 1)
                    for t in range(TB):
                        act.activation(v_f[:, t, :, 0:HD], ps[:, V_BANKS[t], :].rearrange("p (h d) -> p h d", d=HD),
                                       ACT.Copy).then_inc(v_hi, 1)
                elif N_G <= n < N_WO:
                    act.wait_ge(slab_done, n + 1)
                    m, w = (n - N_G) // 2, (n - N_G) % 2
                    act.activation(gates[:, m, w, :], ps[:, b, :], ACT.Copy).then_inc(gate_taken, 1)

            def exps(a):
                b = a % 2
                act.wait_ge(max_done, a + 1)
                if a >= 1:
                    act.wait_ge(probT_done, a)
                if a >= 2:
                    act.wait_ge(norm_done, a - 1)
                if a < 8:
                    j, g = unit_place(a)
                    h = j + 4 * g
                    act.activation(esink[:, b, :], nmax[:, b, :], ACT.Exp, bias=sink_sb[:, h:h + 1])
                for i, (bank, col, w, _, off) in enumerate(score_regions(a)):
                    last = act.activation(prob[:, off:off + w], ps[:, bank, col:col + w], ACT.Exp,
                                          bias=nmax[:, b, i:i + 1], accum_out=den[:, b, i:i + 1])
                last.then_inc(exp_done, 1)

            def take_probT(a):
                act.wait_ge(probT_done, a + 1)
                if a >= 1:
                    act.wait_ge(pv_done, a)
                for k, (bank, w) in enumerate(pt_parts(a)):
                    act.activation(pth[:, 512 * k:512 * k + w], ps[:, bank, 0:w], ACT.Copy).then_inc(probT_hi, 1)

            def take_o_low(a):
                j, g = unit_place(a)
                act.wait_ge(pv_done, a + 1)
                if a >= 1:
                    act.wait_ge(o_sum_done, a)
                act.activation(o_low[half(g), :], ps[half(1), O_BANK, :], ACT.Copy).then_inc(o_low_done, 1)

            def take_o(a):
                j, g = unit_place(a)
                act.wait_ge(o_sum_done, a + 1)
                act.activation((o_s if a < 8 else o_f)[half(g), j, 0, :], o_sum[half(g), :], ACT.Copy)\
                    .then_inc(o_hi, 1)

            def rstd_root(k):
                act.wait_ge(ln_dve, k + 1)
                act.activation(rstd[:, k % 2, 1:2], rstd[:, k % 2, 0:1], ACT.Sqrt).then_inc(ln_act, 1)

            def h_hi(t):
                act.wait_ge(hT_done, t + 1)
                for half in range(2):
                    src = ps[:, WOUT_BANKS[t][half], :].rearrange("p (c q) -> p c q", c=4)
                    act.activation(hTh[:, 4 * half:4 * half + 4, t * P:(t + 1) * P], src, ACT.Copy)\
                        .then_inc(hT_hi, 1)

            for c in range(KC):
                act.wait_ge(x_landed[c], 16)
                act.activation(xh[:, c, :], x_raw[:, c, :], ACT.Copy).then_inc(x_hi, 1)
                if c == 0:
                    slab_hi(0)
            for n in range(1, AHEAD + 1):
                slab_hi(n)
            for n in range(1, N_WOUT + KC - WOUT_TAIL + 1):
                if n - 1 in ROPE_SLABS:
                    rope_rotate(n - 1, ROPE_SLABS.index(n - 1))
                take(n - 1)
                if n == N_VF + 2:
                    act.wait_ge(fg_dve, 3)
                    act.activation(fg[:, 2, :], fg[:, 1, :], ACT.Exp, scale=-1.0).then_inc(fg_act, 1)
                    act.wait_ge(fg_dve, 4)
                    act.activation(fg[:, 4, :], fg[:, 3, :], ACT.Ln).then_inc(fg_act, 1)
                for a in units_at(n, 2):
                    take_o_low(a)
                for a in units_at(n, 0):
                    exps(a)
                for a in units_at(n, 2):
                    take_o(a)
                for a in units_at(n, 1):
                    take_probT(a)
                if N_WO <= n < N_WOUT:
                    m = n - N_WO
                    act.wait_ge(gate_taken, 2 * m + 2)
                    act.activation(gates[:, m, :, :], gates[:, m, :, :], ACT.Sigmoid).then_inc(gate_sig, 1)
                slab_hi(n + AHEAD)
                if n - 1 in ROPE_SLABS:
                    rope_split(n - 1, ROPE_SLABS.index(n - 1))
                if N_WO < n <= N_WOUT:
                    m = n - 1 - N_WO
                    act.wait_ge(merge_sum, m + 1)
                    act.activation(mh[:, m, :], mg[:, m % 2, :], ACT.Copy).then_inc(merge_hi, 1)
            rstd_root(0)
            rstd_root(1)
            h_hi(0)
            for n in range(N_FF, N_FF + 4):
                if n > N_WOUT + KC - WOUT_TAIL + AHEAD:
                    slab_hi(n)
                if n == N_FF + 1:
                    h_hi(1)
            rstd_root(2)
            h_hi(2)
            rstd_root(3)
            h_hi(3)

            def silu(f):
                act.wait_ge(slab_done, N_FF + 2 * f + 1)
                act.activation(sg[:, f % 2, :], ps[:, FF_BANKS[f % 2][0], :], ACT.Silu).then_inc(silu_done, 1)

            for r in range(4):
                if r % 2:
                    silu(r // 2)
                slab_hi(N_FF + r + 4)
            for k in range(2):
                act.wait_ge(ff_done, k + 1)
                act.activation(ah[:, k, :], ffT[:, k, :], ACT.Copy).then_inc(a_hi, 1)

            with act.Fori(1, FT // 2) as i:
                for r in range(4):
                    m = N_FF + r + AHEAD + 1
                    if r % 2:
                        fi = r // 2
                        act.wait_ge(slab_done, i * 4 + (N_FF + r))
                        act.wait_ge(ff_done, i * 2 + (fi - 1))
                        act.activation(sg[:, fi, :], ps[:, FF_BANKS[fi][0], :], ACT.Silu).then_inc(silu_done, 1)
                    act.wait_ge(slab_landed[m % RAW], i * (16 * 4 // RAW) + landed_count(m))
                    act.wait_ge(slab_done, i * 4 + (m - SPL + 1))
                    act.activation(slot(sh, m), raw_of(m), ACT.Copy).then_inc(hi_ready, 1)

            def down_step(i, r, slab, split):
                m = N_DN + r + AHEAD + 1
                if split:
                    act.wait_ge(slab_done, i * 4 + (N_DN + r - 1))
                    act.wait_ge(ff_done, i * 4 + (r + 3))
                    s = (r + 2) % SPL
                    act.activation(ah[:, s:s + 1, :], ffT[:, bass.ds(i * 4 + (r + 2), 1), :], ACT.Copy)\
                        .then_inc(a_hi, 1)
                if slab:
                    act.wait_ge(slab_landed[m % RAW], i * (16 * 4 // RAW) + landed_count(m))
                    act.wait_ge(slab_done, i * 4 + (m - SPL + 1))
                    act.activation(slot(sh, m), raw_of(m), ACT.Copy).then_inc(hi_ready, 1)

            with act.Fori(0, 4) as i:
                for r in range(4):
                    down_step(i, r, True, True)
            for r in range(4):
                down_step(4, r, 16 + r + AHEAD + 1 < FT, 16 + r + 2 < FT)
            for t in range(TB):
                rstd_root(TB + t)

        @block.vector
        def _(dve):
            def slab_lo(n):
                dve.wait_ge(hi_ready, n + 1)
                w = width_of(n)
                dve.tensor_tensor(slot(sl, n, w), raw_of(n), slot(sh, n, w).bitcast(F32),
                                  ALU.subtract).then_inc(lo_ready, 1)

            def low(dst, src, hi):
                return dve.tensor_tensor(dst, src, hi.bitcast(F32), ALU.subtract)

            def rope_cosine(n, k):
                dve.wait_ge(slab_done, n + 1)
                if k == 0:
                    dve.wait_ge(small_landed, 64)
                else:
                    dve.wait_ge(rope_done, k)
                dve.scalar_tensor_tensor(out=rope1[:, :], in0=ps[:, proj_bank(n), :],
                                         scalar=1.0 if n == N_KS else SCALE, in1=cs[:, 0, :],
                                         op0=ALU.mult, op1=ALU.mult).then_inc(rope_cos, 1)

            def rope_finish(n, k):
                dve.wait_ge(rope_sin, k + 1)
                dve.wait_ge(rope_cos, k + 1)
                dve.tensor_tensor(rope1[:, :], rope1[:, :], rope3[:, :], ALU.add).then_inc(rope_sum, 1)
                dve.wait_ge(rope_sum, k + 1)
                dve.wait_ge(rope_hi, k + 1)
                for g in range(2):
                    if n == N_KS:
                        last = low(kl_s[half(g), :], rope1[half(g), :], kh_s[half(g), g, :])
                    else:
                        h = 2 * N_QS.index(n) + g
                        last = low(q_s[half(1 - g), h, :], rope1[half(g), :], q_s[half(g), h, :])
                last.then_inc(rope_done, 1)

            def take(n):
                b = proj_bank(n)
                if n == N_VF:
                    dve.wait_ge(v_hi, 1)
                    for a in range(2):
                        last = low(v_s[:, 2 * a:2 * a + 2, :, HD:2 * HD],
                                   ps[:, 2 + a, 0:2 * VF_W].rearrange("p (b c) -> p b c", b=2)[:, :, 0:KV_W]
                                   .rearrange("p b (g d) -> p b g d", g=2),
                                   v_s[:, 2 * a:2 * a + 2, :, 0:HD])
                    last.then_inc(vs_taken, 1)
                elif N_QF <= n < N_KF:
                    dve.wait_ge(qk_hi, n - N_QF + 1)
                    for g in range(2):
                        h = 2 * (n - N_QF) + g
                        last = dve.scalar_tensor_tensor(
                            out=q_f[half(1 - g), h, :], in0=ps[half(g), b, :], scalar=SCALE,
                            in1=q_f[half(g), h, :].bitcast(F32), op0=ALU.mult, op1=ALU.subtract)
                    last.then_inc(qk_taken, 1)
                elif N_KF <= n < N_V:
                    dve.wait_ge(qk_hi, n - N_QF + 1)
                    for g in range(2):
                        last = low(kl_f[half(g), n - N_KF, :], ps[half(g), b, :], kh_f[half(g), 2 * (n - N_KF) + g, :])
                    last.then_inc(qk_taken, 1)
                elif n == N_G - 1:
                    for t in range(TB):
                        dve.wait_ge(v_hi, t + 2)
                        low(v_f[:, t, :, HD:2 * HD], ps[:, V_BANKS[t], :].rearrange("p (h d) -> p h d", d=HD),
                            v_f[:, t, :, 0:HD]).then_inc(v_taken, 1)

            fgn = [0]

            def fg_step(ins):
                fgn[0] += 1
                ins.then_inc(fg_dve, 1)
                dve.wait_ge(fg_dve, fgn[0])

            def forget_gate_1():
                z, az, e, u, lnu = (fg[:, k, :] for k in range(5))
                dve.wait_ge(slab_done, N_VF + 1)
                logit = ps[:, 2:4, 0:2 * VF_W].rearrange("p a (b c) -> p a b c", b=2)[:, :, :, KV_W:VF_W]
                bf = bf_sb[:, :].unsqueeze(1).unsqueeze(1).broadcast_to([P, 2, 2, HEADS])
                fg_step(dve.tensor_tensor(z.rearrange("p (a b h) -> p a b h", a=2, b=2), logit, bf, ALU.add))
                fg_step(dve.tensor_scalar(az, z, -1.0, None, ALU.mult))
                fg_step(dve.tensor_tensor(az, z, az, ALU.max))

            def forget_gate_2():
                z, az, e, u, lnu, um, d, ru, mn, lf = (fg[:, k, :] for k in range(10))
                dve.wait_ge(fg_act, 1)
                fg_step(dve.tensor_scalar(u, e, 1.0, None, ALU.add))
                fg_step(dve.tensor_scalar(um, u, -1.0, None, ALU.add))
                fg_step(dve.tensor_tensor(d, e, um, ALU.subtract))
                fg_step(dve.reciprocal(ru, u))
                fg_step(dve.tensor_tensor(d, d, ru, ALU.mult))
                fg_step(dve.tensor_scalar(mn, z, 0.0, None, ALU.min))
                fg_step(dve.tensor_tensor(mn, mn, d, ALU.subtract))
                dve.wait_ge(fg_act, 2)
                fg_step(dve.tensor_tensor(lf, mn, lnu, ALU.subtract))

            def bias_stacks():
                dve.wait_ge(cum_done, 1)
                c_sb, c_lo = fg[:, 0, :], fg[:, 1, :]
                fg_step(dve.tensor_copy(c_sb, ps[:, 4, 0:TB * HEADS]))
                fg_step(dve.tensor_copy(c_hi[:, :], c_sb))
                fg_step(dve.tensor_tensor(c_lo, c_sb, c_hi[:, :].bitcast(F32), ALU.subtract))
                dve.wait_ge(consts_made, 4)
                th = lambda ap: ap.rearrange("p (t h) -> p t h", t=TB)
                fg_step(dve.tensor_scalar(stack[:, :, 0:8], th(c_hi[:, :].bitcast(F32)), -1.0, None, ALU.mult))
                fg_step(dve.tensor_scalar(stack[:, :, 8:16], th(c_lo), -1.0, None, ALU.mult))
                fg_step(dve.tensor_copy(stack[:, :, 48:56], th(c_hi[:, :].bitcast(F32))))
                fg_step(dve.tensor_copy(stack[:, :, 56:64], th(c_lo)))

            def take_stacks():
                dve.wait_ge(stackT_done, 1)
                dve.tensor_copy(bias_r[:, :], ps[0:32, 4, :]).then_inc(bias_ready, 1)
                dve.tensor_copy(bias_l32[:, :], ps[32:64, 4, :]).then_inc(bias_ready, 1)

            def head_bias(h):
                dve.wait_ge(bias_ready, 2)
                if h >= 2:
                    dve.wait_ge(scores_done, 8 + h - 1)
                dve.tensor_scalar(bias_l[:, h % 2, :], bias_l32[:, :], sel_sb[:, h:h + 1], None, ALU.mult)\
                    .then_inc(bias_l_ready, 1)

            def maxima(a):
                b = a % 2
                dve.wait_ge(scores_done, a + 1)
                if a >= 2:
                    dve.wait_ge(exp_done, a - 1)
                j, g = unit_place(a)
                for i, (bank, col, w, _, _) in enumerate(score_regions(a)):
                    s = ps[:, bank, col:col + w]
                    if a < 8:
                        dve.tensor_reduce(smax[:, b, i:i + 1], s, AX_X, ALU.max).then_inc(max_part, 1)
                    else:
                        last = dve.tensor_reduce(nmax[:, b, i:i + 1], s, AX_X, ALU.max, negate=True)
                if a < 8:
                    h = j + 4 * g
                    dve.wait_ge(max_part, 4 * (a + 1))
                    last = dve.tensor_scalar(nmax[:, b, :], smax[:, b, :], sink_sb[:, h:h + 1], -1.0,
                                             ALU.max, ALU.mult)
                last.then_inc(max_done, 1)

            def normalise(a):
                b = a % 2
                dve.wait_ge(exp_done, a + 1)
                if a < 8:
                    dve.tensor_tensor(den[:, b, :], den[:, b, :], esink[:, b, :], ALU.add).then_inc(den_part, 1)
                    dve.wait_ge(den_part, a + 1)
                dve.reciprocal(rden[:, b, :], den[:, b, :]).then_inc(rden_done, 1)
                dve.wait_ge(rden_done, a + 1)
                for i, (_, _, w, _, off) in enumerate(score_regions(a)):
                    last = dve.tensor_scalar(prob[:, off:off + w], prob[:, off:off + w],
                                             rden[:, b, i:i + 1], None, ALU.mult)
                last.then_inc(norm_done, 1)

            def take_probT(a):
                for k, (bank, w) in enumerate(pt_parts(a)):
                    dve.wait_ge(probT_hi, probT_parts_before(a) + k + 1)
                    last = low(ptl[:, 512 * k:512 * k + w], ps[:, bank, 0:w], pth[:, 512 * k:512 * k + w])
                last.then_inc(probT_taken, 1)

            def sum_o(a):
                j, g = unit_place(a)
                dve.wait_ge(o_low_done, a + 1)
                if a >= 1:
                    dve.wait_ge(o_lo, a)
                dve.tensor_tensor(o_sum[half(g), :], ps[half(0), O_BANK, :], o_low[half(g), :], ALU.add)\
                    .then_inc(o_sum_done, 1)

            def take_o(a):
                j, g = unit_place(a)
                dst = o_s if a < 8 else o_f
                dve.wait_ge(o_hi, a + 1)
                dve.wait_ge(o_sum_done, a + 1)
                low(dst[half(g), j, 1, :], o_sum[half(g), :], dst[half(g), j, 0, :]).then_inc(o_lo, 1)

            def merge(m):
                b = 2 + 2 * (m % 2)
                dve.wait_ge(slab_done, N_WO + m + 1)
                dve.wait_ge(gate_sig, m + 1)
                if m >= 1:
                    dve.wait_ge(merge_sum, m)
                dve.tensor_tensor(mt1[:, :], gates[:, m, 0, :], ps[:, b, :], ALU.mult).then_inc(merge_part, 1)
                dve.tensor_tensor(mt2[:, :], gates[:, m, 1, :], ps[:, b + 1, :], ALU.mult).then_inc(merge_taken, 1)
                dve.wait_ge(merge_part, m + 1)
                dve.wait_ge(merge_taken, m + 1)
                if m >= 2:
                    dve.wait_ge(merge_hi, m - 1)
                dve.tensor_tensor(mg[:, m % 2, :], mt1[:, :], mt2[:, :], ALU.add).then_inc(merge_sum, 1)

            def merge_low(m):
                dve.wait_ge(merge_hi, m + 1)
                dve.tensor_tensor(ml[:, m, :], mg[:, m % 2, :], mh[:, m, :].bitcast(F32), ALU.subtract)\
                    .then_inc(merge_lo, 1)

            steps = [0]

            def signal(ins):
                ins.then_inc(ln_part, 1)
                steps[0] += 1
                return steps[0]

            def layer_norm(k):
                ln, t, s = k // TB, k % TB, k % 2
                banks = (WOUT_BANKS, DN_BANKS)[ln][t]
                params = (ln1p, ln2p)[ln]
                cols = [slice(512 * q, 512 * q + 512) for q in range(2)]
                if k == 0:
                    dve.wait_ge(res_landed, 48)
                if k == TB:
                    dve.wait_ge(ln2_landed, 32)
                if ln:
                    dve.wait_ge(ln_done, t + 1)

                def residual(q):
                    if k == TB - 1:
                        dve.wait_ge(slab_done, N_FF)
                    else:
                        dve.wait_ge(block_done, 2 * (k - (k >= TB)) + q + 1)
                    r = res[:, t, cols[q]]
                    return signal(dve.scalar_tensor_tensor(out=r, in0=r, scalar=ALPHA, in1=ps[:, banks[q], :],
                                                           op0=ALU.mult, op1=ALU.add))

                def statistics(q, after):
                    dve.wait_ge(ln_part, after)
                    return signal(dve.bn_stats(stats[:, s, 6 * q:6 * q + 6], res[:, t, cols[q]]))

                if k == 2 * TB - 1:
                    statistics(0, residual(0))
                    n = statistics(1, residual(1))
                else:
                    first, second = residual(0), residual(1)
                    statistics(0, first)
                    n = statistics(1, second)
                dve.wait_ge(ln_part, n)
                mean, v = mv[:, s, 0:1], rstd[:, s, 0:1]
                n = signal(dve.bn_aggr(mv[:, s, :], stats[:, s, :]))
                dve.wait_ge(ln_part, n)
                dve.tensor_scalar(v, mv[:, s, 1:2], LN_EPS, None, ALU.add).then_inc(ln_dve, 1)
                scaled = []
                for q in range(2):
                    r = res[:, t, cols[q]]
                    scaled.append(signal(dve.scalar_tensor_tensor(out=r, in0=r, scalar=mean,
                                                                  in1=params[:, 0, cols[q]],
                                                                  op0=ALU.subtract, op1=ALU.mult)))
                root, r0, tmp = (rstd[:, s, q:q + 1] for q in range(1, 4))
                dve.wait_ge(ln_act, k + 1)
                dve.wait_ge(ln_part, signal(dve.reciprocal(r0, root)))
                dve.wait_ge(ln_part, signal(dve.scalar_tensor_tensor(out=tmp, in0=r0, scalar=v, in1=r0,
                                                                     op0=ALU.mult, op1=ALU.mult)))
                dve.wait_ge(ln_part, signal(dve.tensor_scalar(tmp, tmp, -0.5, 1.5, ALU.mult, ALU.add)))
                dve.wait_ge(ln_part, signal(dve.tensor_tensor(r0, r0, tmp, ALU.mult)))
                for q in range(2):
                    r = res[:, t, cols[q]]
                    ins = dve.scalar_tensor_tensor(out=r, in0=r, scalar=r0, in1=params[:, 1, cols[q]],
                                                   op0=ALU.mult, op1=ALU.add)
                    if ln or q:
                        ins.then_inc(ln_done, 1)

            def h_lo(t):
                tok = slice(t * P, (t + 1) * P)
                for q in range(2):
                    dve.wait_ge(hT_hi, 2 * t + q + 1)
                    src = ps[:, WOUT_BANKS[t][q], :].rearrange("p (c q) -> p c q", c=4)
                    last = low(hTl[:, 4 * q:4 * q + 4, tok], src, hTh[:, 4 * q:4 * q + 4, tok])
                last.then_inc(hT_ready, 1)

            for c in range(KC):
                dve.wait_ge(x_hi, c + 1)
                dve.tensor_tensor(xl[:, c, :], x_raw[:, c, :], xh[:, c, :].bitcast(F32), ALU.subtract)\
                    .then_inc(x_lo, 1)
                if c == 0:
                    slab_lo(0)
            for n in range(1, AHEAD + 1):
                slab_lo(n)
            for n in range(1, N_WOUT + KC - WOUT_TAIL + 1):
                if n - 1 in ROPE_SLABS:
                    rope_cosine(n - 1, ROPE_SLABS.index(n - 1))
                if n == N_VF + 1:
                    forget_gate_1()
                if n == N_VF + 2:
                    forget_gate_2()
                take(n - 1)
                for a in units_at(n, 2):
                    sum_o(a)
                for a in units_at(n, 0):
                    maxima(a)
                if n == N_QF:
                    bias_stacks()
                if n == N_QF + 1:
                    take_stacks()
                for a in units_at(n + 1, 0):
                    if a >= 8:
                        head_bias(a - 8)
                for a in units_at(n, 0):
                    normalise(a)
                for a in units_at(n, 2):
                    take_o(a)
                for a in units_at(n, 1):
                    take_probT(a)
                if N_WO < n <= N_WOUT:
                    merge(n - 1 - N_WO)
                slab_lo(n + AHEAD)
                if n - 1 in ROPE_SLABS:
                    rope_finish(n - 1, ROPE_SLABS.index(n - 1))
                if N_WO < n <= N_WOUT:
                    merge_low(n - 1 - N_WO)
            layer_norm(0)
            layer_norm(1)
            h_lo(0)
            slab_lo(N_FF)
            slab_lo(N_FF + 1)
            h_lo(1)
            layer_norm(2)
            layer_norm(3)
            h_lo(2)
            h_lo(3)

            def hidden(f):
                dve.wait_ge(silu_done, f + 1)
                dve.wait_ge(slab_done, N_FF + 2 * f + 2)
                dve.tensor_tensor(ffT[:, f, :], sg[:, f, :], ps[:, FF_BANKS[f][1], :], ALU.mult).then_inc(ff_done, 1)

            for r in range(4):
                if r % 2:
                    hidden(r // 2)
                slab_lo(N_FF + r + 4)
            for k in range(2):
                dve.wait_ge(a_hi, k + 1)
                low(al[:, k, :], ffT[:, k, :], ah[:, k, :]).then_inc(a_lo, 1)
            with dve.Fori(1, FT // 2) as i:
                for r in range(4):
                    m = N_FF + r + AHEAD + 1
                    if r % 2:
                        fi = r // 2
                        dve.wait_ge(silu_done, i * 2 + (fi + 1))
                        dve.wait_ge(slab_done, i * 4 + (N_FF + r + 1))
                        dve.tensor_tensor(ffT[:, bass.ds(i * 2 + fi, 1), :], sg[:, fi:fi + 1, :],
                                          ps[:, FF_BANKS[fi][1]:FF_BANKS[fi][1] + 1, :], ALU.mult)\
                            .then_inc(ff_done, 1)
                    dve.wait_ge(hi_ready, i * 4 + (m + 1))
                    low(slot(sl, m), raw_of(m), slot(sh, m)).then_inc(lo_ready, 1)

            def down_step(i, r, slab, split):
                m = N_DN + r + AHEAD + 1
                if split:
                    dve.wait_ge(a_hi, i * 4 + (r + 3))
                    s = (r + 2) % SPL
                    low(al[:, s:s + 1, :], ffT[:, bass.ds(i * 4 + (r + 2), 1), :], ah[:, s:s + 1, :])\
                        .then_inc(a_lo, 1)
                if slab:
                    dve.wait_ge(hi_ready, i * 4 + (m + 1))
                    low(slot(sl, m), raw_of(m), slot(sh, m)).then_inc(lo_ready, 1)

            with dve.Fori(0, 4) as i:
                for r in range(4):
                    down_step(i, r, True, True)
            for r in range(4):
                down_step(4, r, 16 + r + AHEAD + 1 < FT, 16 + r + 2 < FT)
            for t in range(TB):
                layer_norm(TB + t)

        @block.tensor
        def _(pe):
            def mm3(dst, lh, ll, rh, rl, start, stop):
                pe.matmul(dst, lh, rh, start=start, stop=False)
                pe.matmul(dst, ll, rh, start=False, stop=False)
                return pe.matmul(dst, lh, rl, start=False, stop=stop)

            def cut(n, a, b):
                s = (n % SPL) * D
                return sh[:, s + a:s + b], sl[:, s + a:s + b]

            def scores(a):
                u = a % 8
                j, g = unit_place(a)
                regions = score_regions(a)
                q, kh = (q_s[:, u, :], kh_s[:, g, :]) if a < 8 else (q_f[:, u, :], kh_f[:, u, :])
                kl = kl_s[half(g), :] if a < 8 else kl_f[half(g), j, :]
                if a == 0:
                    pe.wait_ge(vs_taken, 1)
                    pe.wait_ge(consts_made, 9)
                elif a == 8:
                    pe.wait_ge(v_taken, TB)
                    pe.wait_ge(qk_taken, 8)
                else:
                    pe.wait_ge(exp_done, a)
                if a < 8:
                    pe.wait_ge(rope_done, 2 + j)
                else:
                    pe.wait_ge(bias_l_ready, u + 1)
                seen = set()
                for i, (bank, col, w, k0, _) in enumerate(regions):
                    pe.matmul(ps[:, bank, col:col + w], q[:, i * P:(i + 1) * P], kh[:, k0 * P:k0 * P + w],
                              start=bank not in seen, stop=False, skip_group_check=True)
                    seen.add(bank)
                for i, (bank, col, w, k0, _) in enumerate(regions):
                    pe.matmul(ps[:, bank, col:col + w], q[half(g), i * P:(i + 1) * P], kl[:, k0 * P:k0 * P + w],
                              start=False, stop=False, skip_group_check=True)
                if a >= 8:
                    for i, (bank, col, w, _, _) in enumerate(regions):
                        pe.matmul(ps[:, bank, col:col + w], bias_l[:, a % 2, i * P:(i + 1) * P], bias_r[:, 0:w],
                                  start=False, stop=False, skip_group_check=True)
                for i, (bank, col, w, _, _) in enumerate(regions):
                    mw = min(w, 2 * P) if a < 8 else P
                    last = pe.matmul(ps[:, bank, col + w - mw:col + w], ident_b[:, :], mask_b[:, 2 * P - mw:2 * P],
                                     start=False, stop=True, skip_group_check=True)
                last.then_inc(scores_done, 1)

            def transposes(a):
                pe.wait_ge(norm_done, a + 1)
                if a >= 1:
                    pe.wait_ge(probT_taken, a)
                keys = key_regions(a)
                for i, (_, _, w, _, off) in enumerate(score_regions(a)):
                    k0 = i + 1 - w // P
                    for kb in range(k0, i + 1):
                        col = keys[kb][0] + (i - kb) * P
                        last = pe.transpose(ps[:, 5 + col // 512, col % 512:col % 512 + P],
                                            prob[:, off + (kb - k0) * P:off + (kb - k0 + 1) * P], ident[:, :])
                last.then_inc(probT_done, 1)

            def values(a):
                _, g = unit_place(a)
                pe.wait_ge(probT_taken, a + 1)
                if a >= 1:
                    pe.wait_ge(o_sum_done, a)
                for kb, (col, w) in enumerate(key_regions(a)):
                    v = v_s[:, kb, g, :] if a < 8 else v_f[:, kb, a - 8, :]
                    for part in (pth, ptl):
                        last = pe.matmul(ps[:, O_BANK, kb * P:kb * P + w], v, part[:, col:col + w],
                                         start=(kb == 0 and part is pth), stop=(kb == TB - 1 and part is ptl),
                                         skip_group_check=True)
                last.then_inc(pv_done, 1)

            def cumulative():
                pe.wait_ge(fg_dve, 11)
                pe.wait_ge(consts_made, 9)
                lf = fg[:, 9, :]
                for t in range(TB):
                    dst = ps[:, 4, t * HEADS:(t + 1) * HEADS]
                    for s in range(t):
                        pe.matmul(dst, ones[:, :], lf[:, s * HEADS:(s + 1) * HEADS], start=(s == 0), stop=False)
                    last = pe.matmul(dst, tri[:, :], lf[:, t * HEADS:(t + 1) * HEADS], start=(t == 0), stop=True)
                last.then_inc(cum_done, 1)

            def stacks():
                pe.wait_ge(fg_dve, 18)
                for t in range(TB):
                    last = pe.transpose(ps[0:64, 4, t * P:(t + 1) * P], stack[:, t, :], ident[:, :])
                last.then_inc(stackT_done, 1)

            def bank_free(n):
                if n in (2, 4, 5, 6, 7):
                    pe.wait_ge(rope_rot, {2: 1, 4: 3, 5: 2, 6: 4, 7: 5}[n])
                elif 8 <= n < N_V:
                    pe.wait_ge(qk_taken, n - 7)
                elif n == N_V:
                    pe.wait_ge(exp_done, 8)
                    pe.wait_ge(bias_ready, 2)
                    pe.wait_ge(qk_taken, 7)
                elif n == N_G:
                    pe.wait_ge(qk_taken, 8)
                elif N_G < n < 30:
                    pe.wait_ge(gate_taken, n - N_G)
                elif n == 30:
                    pe.wait_ge(o_sum_done, UNITS)
                elif n < N_WO and n > 30:
                    pe.wait_ge(gate_taken, n - N_G - 1)
                elif n in (N_WO, N_WO + 1):
                    pe.wait_ge(exp_done, UNITS)
                    pe.wait_ge(probT_taken, UNITS)
                elif N_WO + 2 <= n < N_WOUT:
                    pe.wait_ge(merge_taken, n - N_WO - 1)

            def slab(n, between):
                pe.wait_ge(lo_ready, n + 1)
                bank_free(n)
                b = proj_bank(n)
                if n == N_VF:
                    for t in range(TB):
                        dst = ps[:, 2 + t // 2, (t % 2) * VF_W:(t % 2 + 1) * VF_W]
                        for c in range(KC):
                            tok = slice(t * P, (t + 1) * P)
                            last = mm3(dst, xh[:, c, tok], xl[:, c, tok], *cut(n, c * VF_W, (c + 1) * VF_W),
                                       start=(c == 0), stop=(c == KC - 1))
                elif N_V <= n < N_G:
                    for t in range(TB):
                        if t == 1:
                            between()
                        for i in range(2):
                            c = 2 * (n - N_V) + i
                            tok = slice(t * P, (t + 1) * P)
                            last = mm3(ps[:, V_BANKS[t], :], xh[:, c, tok], xl[:, c, tok],
                                       *cut(n, i * FOX_W, (i + 1) * FOX_W), start=(c == 0), stop=(c == KC - 1))
                elif n < N_WO:
                    for c in range(KC):
                        if n == 0:
                            pe.wait_ge(x_lo, c + 1)
                        if c == 2:
                            between()
                        last = mm3(ps[:, b, :], *cut(n, c * P, (c + 1) * P), xh[:, c, :], xl[:, c, :],
                                   start=(c == 0), stop=(c == KC - 1))
                else:
                    pe.wait_ge(o_lo, UNITS)
                    b = 2 + 2 * (n % 2)
                    for c in range(8):
                        o = o_f[:, c, :, :] if c < 4 else o_s[:, c - 4, :, :]
                        last = mm3(ps[:, b + c // 4, :], *cut(n, c * P, (c + 1) * P), o[:, 0, :], o[:, 1, :],
                                   start=(c % 4 == 0), stop=(c % 4 == 3))
                last.then_inc(slab_done, 1)

            def rows(n, c, lhs, bank, q, t, start, stop):
                return mm3(ps[:, bank, :], *lhs(c, t), *cut(n, 512 * q, 512 * q + 512), start=start, stop=stop)

            def merged(c, t):
                return mh[:, c, t * P:(t + 1) * P], ml[:, c, t * P:(t + 1) * P]

            def turn(n):
                for a in units_at(n, 1):
                    transposes(a)

            for n in range(N_WOUT):
                for a in units_at(n, 0):
                    scores(a)
                for a in units_at(n, 2):
                    values(a)
                if n == N_QF:
                    cumulative()
                if n == N_QF + 1:
                    stacks()
                slab(n, lambda: turn(n))

            def by_blocks(n0, first, count, lhs, banks, slab_wait, hook, signal_slabs):
                end = first + count - 1
                for t in range(TB):
                    slabwise = t == 0 or (signal_slabs and t == TB - 1)
                    order = [(c, q) for c in range(first, end + 1) for q in range(2)]
                    if not slabwise:
                        order.sort(key=lambda cq: (cq[1], cq[0]))
                    for c, q in order:
                        if t == 0 and q == 0:
                            slab_wait(c)
                        if q == 0:
                            hook(t, c)
                        last = rows(n0 + c, c, lhs, banks[t][q], q, t, start=False, stop=(c == end))
                        if signal_slabs and t == TB - 1:
                            if q == 1:
                                last.then_inc(slab_done, 1)
                        elif c == end:
                            last.then_inc(block_done, 1)

            for c in range(KC - WOUT_TAIL):
                n = N_WOUT + c
                pe.wait_ge(lo_ready, n + 1)
                pe.wait_ge(merge_lo, c + 1)
                for t in range(TB):
                    if c == 0 and t == 1:
                        pe.wait_ge(gate_taken, 16)
                    if c == 0 and t >= 2:
                        pe.wait_ge(merge_taken, 5 + t)
                    for q in range(2):
                        last = rows(n, c, merged, WOUT_BANKS[t][q], q, t, start=(c == 0), stop=False)
                last.then_inc(slab_done, 1)

            def turn_h(t):
                pe.wait_ge(ln_done, t + 1)
                for c in range(KC):
                    last = pe.transpose(ps[:, WOUT_BANKS[t][c // 4], (c % 4) * P:(c % 4 + 1) * P],
                                        res[:, t, c * P:(c + 1) * P], ident[:, :])
                last.then_inc(hT_done, 1)

            def wait_wout(c):
                pe.wait_ge(lo_ready, N_WOUT + c + 1)
                pe.wait_ge(merge_lo, c + 1)

            def between_wout(t, c):
                if t == TB - 1 and c == KC - WOUT_TAIL:
                    turn_h(0)
                if t == TB - 1 and c == KC - 1:
                    turn_h(1)

            by_blocks(N_WOUT, KC - WOUT_TAIL, WOUT_TAIL, merged, WOUT_BANKS, wait_wout, between_wout, True)

            def ff_slab(n, f, w, tokens, signal):
                for c in range(KC):
                    last = mm3(ps[:, FF_BANKS[f % 2][w], tokens], *cut(n, c * P, (c + 1) * P),
                               hTh[:, c, tokens], hTl[:, c, tokens], start=(c == 0), stop=(c == KC - 1))
                if signal:
                    last.then_inc(slab_done, 1)

            pe.wait_ge(hT_ready, 2)
            for r in range(4):
                pe.wait_ge(lo_ready, N_FF + r + 1)
                ff_slab(N_FF + r, r // 2, r % 2, slice(0, 2 * P), False)
                if r == 1:
                    turn_h(2)
            turn_h(3)
            pe.wait_ge(hT_ready, 4)
            for r in range(4):
                ff_slab(N_FF + r, r // 2, r % 2, slice(2 * P, SEQ), True)
            with pe.Fori(1, FT // 2) as i:
                for r in range(4):
                    n = N_FF + r
                    pe.wait_ge(lo_ready, i * 4 + (n + 1))
                    if r % 2 == 0:
                        pe.wait_ge(ff_done, i * 2 + (r // 2 - 1))
                    ff_slab(n, r // 2, r % 2, slice(0, SEQ), True)

            def hidden(c, t):
                s = c % SPL
                return ah[:, s, t * P:(t + 1) * P], al[:, s, t * P:(t + 1) * P]

            def down(i, r, peel):
                n = N_DN + r
                pe.wait_ge(lo_ready, i * 4 + (n + 1))
                pe.wait_ge(a_lo, i * 4 + (r + 1))
                for t in range(TB):
                    if peel and t >= 2:
                        pe.wait_ge(ff_done, FT + t - 3)
                    for q in range(2):
                        last = rows(n, r, hidden, DN_BANKS[t][q], q, t, start=peel, stop=False)
                last.then_inc(slab_done, 1)

            for r in range(4):
                down(0, r, r == 0)
            with pe.Fori(1, 4) as i:
                for r in range(4):
                    down(i, r, False)
            for r in range(FT - DN_TAIL - 16):
                down(4, r, False)

            def wait_down(c):
                pe.wait_ge(lo_ready, N_DN + c + 1)
                pe.wait_ge(a_lo, c + 1)

            by_blocks(N_DN, FT - DN_TAIL, DN_TAIL, hidden, DN_BANKS, wait_down, lambda t, c: None, False)


def rope_table():
    half = HD // 2
    freq = (np.float32(10000.0) ** (-np.arange(half, dtype=np.float32) / np.float32(half))).astype(np.float32)
    ang = (np.arange(SEQ, dtype=np.float32)[None, :] * freq[:, None]).astype(np.float32)
    cos, sin = np.cos(ang).astype(np.float32), np.sin(ang).astype(np.float32)
    return np.ascontiguousarray(np.stack([np.concatenate([cos] * 4), np.concatenate([-sin, sin] * 2)], axis=1))


def head_selector():
    return (np.arange(32)[:, None] % HEADS == np.arange(HEADS)[None, :]).astype(np.float32)


def lay_out_slabs(w_in, w_o_fox, w_o_swa, w_out, w_gate, w_up, w_down):
    cols = np.cumsum([FOX_W, FOX_W, FOX_W, HEADS, FOX_W, KV_W, KV_W, D, D])
    qf, kf, vf, fl, qs, ks, vs, gf, gs = np.split(w_in, cols[:-1], axis=1)

    def by_columns(w):
        n = w.shape[1] // P
        return w.reshape(KC, P, n, P).transpose(2, 1, 0, 3).reshape(n, P, D)

    qs = qs.reshape(D, 2, 4, HD).transpose(0, 2, 1, 3).reshape(D, FOX_W)
    os_ = w_o_swa.reshape(2, 4, HD, D).transpose(1, 0, 2, 3).reshape(FOX_W, D)
    qs, ks = by_columns(qs), by_columns(ks)
    v = vf.reshape(4, 2, P, FOX_W).transpose(0, 2, 1, 3).reshape(4, P, D)
    gates = np.stack([by_columns(gf), by_columns(gs)], axis=1).reshape(16, P, D)
    wo = by_columns(np.concatenate([w_o_fox, os_]))
    ff = np.stack([by_columns(w_gate), by_columns(w_up)], axis=1).reshape(2 * FT, P, D)
    slabs = np.concatenate([ks, qs[:2], qs[2:], by_columns(qf), by_columns(kf), v, gates, wo,
                            w_out.reshape(KC, P, D), ff, w_down.reshape(FT, P, D)])
    vs_f = np.concatenate([vs, fl], axis=1).reshape(KC, P, VF_W).transpose(1, 0, 2).reshape(P, KC * VF_W)
    return np.ascontiguousarray(slabs), np.ascontiguousarray(vs_f)


def kernel(**inputs):
    import concourse.bacc as bacc
    from concourse.bass_utils import run_bass_kernel_spmd

    a = {k: np.asarray(v) for k, v in inputs.items()}
    slabs, vf = lay_out_slabs(*(a[k][0] for k in ("w_in", "w_o_fox", "w_o_swa", "w_out", "w_gate", "w_up", "w_down")))
    arrays = {
        "xT": np.ascontiguousarray(a["x"][0].T.reshape(KC, P, SEQ)),
        "x": np.ascontiguousarray(a["x"][0]),
        "slabs": slabs,
        "vf_slab": vf,
        "rope": rope_table(),
        "sel": head_selector(),
        "b_forget": np.ascontiguousarray(a["b_forget"][0]),
        "sinks": np.ascontiguousarray(a["attn_sinks"][0]),
        "ln1_g": np.ascontiguousarray(a["ln1_g"][0]),
        "ln1_b": np.ascontiguousarray(a["ln1_b"][0]),
        "ln2_g": np.ascontiguousarray(a["ln2_g"][0]),
        "ln2_b": np.ascontiguousarray(a["ln2_b"][0]),
    }
    nc = bacc.Bacc("TRN2", target_bir_lowering=False, num_devices=1)
    args = [nc.dram_tensor(f"in_{k}", v.shape, mybir.dt.from_np(v.dtype), kind="ExternalInput").ap()
            for k, v in arrays.items()]
    out = nc.dram_tensor("out_0", (SEQ, D), F32, kind="ExternalOutput").ap()
    program(nc, *args, out)
    r = run_bass_kernel_spmd(nc, [{f"in_{k}": v for k, v in arrays.items()}], core_ids=[0])
    return r.results[0]["out_0"].reshape(1, SEQ, D)
```

```python
from contextlib import ExitStack

import numpy as np

import concourse.bass as bass
from concourse import mybir

ALU = mybir.AluOpType
ACT = mybir.ActivationFunctionType
F32 = mybir.dt.float32
F32R = mybir.dt.float32r
BF16 = mybir.dt.bfloat16
AX_X = mybir.AxisListType.X

P = 128
SEQ = 512
D = 1024
D_FF = 2816
HD = 64
HEADS = 8
FOX_W = HEADS * HD
KV_W = 2 * HD
ALPHA = 2.0 ** 0.25
LN_EPS = 1e-5
SCALE = 1.0 / HD ** 0.5
NEG = -1.0e30
TB = SEQ // P
KC = D // P
FT = D_FF // P

N_QS = (0, 1, 4, 5)
N_VK = (2, 3)
N_QF = 6
N_KF = 10
N_V = 14
N_G = 18
N_WO = 34
N_WOUT = 42
N_FF = 50
N_DN = N_FF + 2 * FT
SLABS = N_DN + FT
VK_W = 2 * KV_W + HEADS
FIRST = 4
RAW = 2
SPL = 4
AHEAD = SPL - 1
LATE = (N_FF, N_FF + 1, N_FF + 2)

PART = (slice(0, D // 2), slice(D // 2, D))
POOL_LO = (*range(10, 17), *range(N_FF, N_FF + 3))
WOUT_TAIL = 4
DN_TAIL = 4
UNITS = 16
N_CUM = 16
LAST_LN = 2 * TB - 1
WARM_UP = 9

ROPE_BANKS = (7, 0, 6, 5)
VK_BANKS = slice(1, 5)
K_BANK = 7
C_BANK = 0
V_BANKS = (2, 3, 4, 7)
O_BANK = 1
WOUT_BANKS = ((6, 7), (0, 1), (2, 3), (4, 5))
DN_BANKS = ((2, 3), (4, 5), (6, 7), (0, 1))
FF_BANKS = ((6, 7), (0, 1))


def unit_step(a):
    return 6 + a if a < 8 else 19 + a - 8


def units_at(n, stage):
    return [a for a in range(UNITS) if unit_step(a) + stage == n]


def proj_bank(n):
    if n in N_QS:
        return ROPE_BANKS[N_QS.index(n)]
    if n < N_V:
        return 0 if n % 2 else 7
    return {27: 2, 28: 3, 30: 1, 32: 1}.get(n, 0)


def score_regions(a):
    if a < 8:
        return [(2, 0, 128, 0, 0), (2, 128, 256, 0, 128), (3, 0, 256, 1, 384), (3, 256, 256, 2, 640)]
    return [(2, 0, 128, 0, 0), (3, 0, 256, 0, 128), (2, 128, 384, 0, 384), (4, 0, 512, 0, 768)]


def key_regions(a):
    if a < 8:
        return [(0, 256), (256, 256), (512, 256), (768, 128)]
    return [(0, 512), (512, 384), (1024, 256), (896, 128)]


def pt_parts(a):
    return [(5, 512), (6, 384)] if a < 8 else [(5, 512), (6, 512), (7, 256)]


def probT_parts_before(a):
    return sum(len(pt_parts(b)) for b in range(a))


def half(g):
    return slice(g * HD, (g + 1) * HD)


def bias_rows(g):
    return slice((1 - g) * HD, (1 - g) * HD + 32)


def zero_rows(g):
    return slice((1 - g) * HD + 32, (1 - g) * HD + HD)


def unit_place(a):
    u = a % 8
    return u // 2, u % 2


def program(nc, xT, x, slabs, vk_slabs, rope, rope_tok, sel, b_forget, sinks, ln1_g, ln1_b, ln2_g, ln2_b, out):
    ctx = ExitStack()
    with ctx:
        base = -(-nc.sbuf_base // 64) * 64

        def at(name, kb, shape, dt=F32):
            return nc.alloc_sbuf_tensor_at(name, shape, dt, offset=base + int(kb * 1024))

        def sem(name):
            return ctx.enter_context(nc.semaphore(name))

        xh = at("xh", 0, [P, KC, SEQ], F32R)
        xl = at("xl", 16, [P, KC, SEQ], F32R)
        mh = at("mh", 0, [P, KC, SEQ], F32R)
        ml = at("ml", 16, [P, KC, SEQ], F32R)
        ah = at("ah", 0, [P, SPL, SEQ], F32R)
        al = at("al", 8, [P, SPL, SEQ], F32R)
        sg = at("sg", 16, [P, 2, SEQ])
        ln2p = at("ln2p", 20, [P, 2, D])
        x_raw = at("x_raw", 32, [P, KC, SEQ])
        q_s = at("q_s", 32, [P, HEADS, SEQ], F32R)
        kh_s = at("kh_s", 48, [P, 2, SEQ], F32R)
        kl_s = at("kl_s", 52, [P, SEQ], F32R)
        v_s = at("v_s", 54, [P, TB, 2, 2 * HD], F32R)
        rope1 = [at("rope1_even", 58, [P, SEQ]), at("rope1_odd", 134, [P, SEQ])]
        rope2 = at("rope2", 60, [P, SEQ])
        rope3 = at("rope3", 62, [P, SEQ])
        gates = at("gates", 32, [P, KC, 2, SEQ])
        hTh = at("hTh", 32, [P, KC, SEQ], F32R)
        hTl = at("hTl", 48, [P, KC, SEQ], F32R)
        q_aug = at("q_aug", 56, [P, 2, SEQ], F32R)
        k_aug = at("k_aug", 60, [P, 2, SEQ], F32R)
        kh_f = at("kh_f", 64, [P, HEADS, SEQ], F32R)
        kl_f = at("kl_f", 80, [P, 4, SEQ], F32R)
        q_f = at("q_f", 88, [P, HEADS, SEQ], F32R)
        v_f = at("v_f", 104, [P, TB, HEADS, 2 * HD], F32R)
        o_f = at("o_f", 88, [P, 4, 2, SEQ], F32R)
        o_s = at("o_s", 120, [P, 4, 2, SEQ], F32R)
        res = at("res", 64, [P, TB, D])
        ln1p = at("ln1p", 80, [P, 2, D])
        ffT = at("ffT", 88, [P, FT, SEQ])
        first_raw = at("first_raw", 104, [P, FIRST, KC // 2 * VK_W])
        k_rot = at("k_rot", 136, [P, TB, 2, 2, HD // 2])
        k_sin = at("k_sin", 138, [P, TB, 2, 2, HD // 2])
        cs_tok = at("cs_tok", 140, [P, TB, 2, HD // 2])
        prob = at("prob", 136, [P, 1280])
        pth = at("pth", 141, [P, 1280], F32R)
        ptl = at("ptl", 146, [P, 1280], F32R)
        mt1 = at("mt1", 136, [P, SEQ])
        mt2 = at("mt2", 138, [P, SEQ])
        mg = at("mg", 140, [P, 2, SEQ])
        late_raw = at("late_raw", 136, [P, len(LATE), D])
        raw = at("raw", 151, [P, RAW * D])
        sh = at("sh", 159, [P, SPL * D + 64], F32R)
        sl = at("sl", 175.25, [P, SPL * D + 64], F32R)
        cs = at("cs", 191.5, [P, 2, SEQ])
        bias_l32 = at("bias_l32", 191.5, [32, SEQ])
        tri = at("tri", 195.5, [P, P])
        ones = at("ones", 196, [P, P])
        stack = at("stack", 196.5, [P, TB, 64])
        ident = at("ident", 199.5, [P, P])
        ident_b = at("ident_b", 200, [P, P], BF16)
        mask_b = at("mask_b", 200.25, [P, 2 * P], BF16)
        o_low = at("o_low", 200.75, [P, SEQ])
        o_sum = at("o_sum", 202.75, [P, SEQ])
        sel_sb = at("sel_sb", 204.75, [32, HEADS])
        bf_sb = at("bf_sb", 204.8125, [P, HEADS])
        sink_sb = at("sink_sb", 204.875, [P, HEADS])
        fg = at("fg", 205, [P, 10, TB * HEADS])
        c_hi = at("c_hi", 206.25, [P, TB * HEADS], F32R)
        nmax = at("nmax", 206.375, [P, 2, 4])
        smax = at("smax", 206.4375, [P, 2, 4])
        den = at("den", 206.5, [P, 2, 4])
        esink = at("esink", 206.5625, [P, 2, 4])
        rden = at("rden", 206.625, [P, 2, 4])
        stats = at("stats", 206.6875, [P, 2, 12])
        mv = at("mv", 206.8125, [P, 2, 2])
        rstd = at("rstd", 206.84375, [P, 2, 4])
        eps_sb = at("eps_sb", 206.90625, [P, 1])
        warm = at("warm", 206.9375, [P, 1])

        ps = ctx.enter_context(nc.psum_tensor("ps", [P, 8, 512], F32))

        x_landed = [sem(f"x_landed{c}") for c in range(KC)]
        part_landed = [sem(f"part_landed{k}") for k in range(4)]
        part_hi = sem("part_hi")
        part_lo = sem("part_lo")
        first_landed = {n: sem(f"first_landed{n}") for n in range(2, FIRST)}
        slab_landed = [sem(f"slab_landed{r}") for r in range(RAW)]
        cs_landed = sem("cs_landed")
        cs_tok_landed = sem("cs_tok_landed")
        late_landed = [sem(f"late_landed{k}") for k in range(len(LATE))]
        small_landed = sem("small_landed")
        res_landed = sem("res_landed")
        ln2_landed = sem("ln2_landed")
        consts_made = sem("consts_made")
        x_hi = sem("x_hi")
        x_lo = sem("x_lo")
        hi_ready = sem("hi_ready")
        lo_ready = sem("lo_ready")
        slab_done = sem("slab_done")
        rope_rot = sem("rope_rot")
        rope_cos = sem("rope_cos")
        rope_sin = sem("rope_sin")
        rope_sum = sem("rope_sum")
        rope_hi = sem("rope_hi")
        rope_done = sem("rope_done")
        k_part = sem("k_part")
        k_rotated = sem("k_rotated")
        kT_done = sem("kT_done")
        kT_hi = sem("kT_hi")
        ks_taken = sem("ks_taken")
        vs_hi = sem("vs_hi")
        vs_taken = sem("vs_taken")
        qk_hi = sem("qk_hi")
        qk_taken = sem("qk_taken")
        v_hi = sem("v_hi")
        v_taken = sem("v_taken")
        gate_taken = sem("gate_taken")
        fg_dve = sem("fg_dve")
        fg_act = sem("fg_act")
        cum_done = sem("cum_done")
        stackT_done = sem("stackT_done")
        bias_ready = sem("bias_ready")
        bias_l_ready = sem("bias_l_ready")
        zeros_made = sem("zeros_made")
        aug_ready = sem("aug_ready")
        scores_done = sem("scores_done")
        max_part = sem("max_part")
        max_done = sem("max_done")
        exp_done = sem("exp_done")
        den_part = sem("den_part")
        rden_done = sem("rden_done")
        norm_done = sem("norm_done")
        probT_done = sem("probT_done")
        probT_hi = sem("probT_hi")
        probT_taken = sem("probT_taken")
        pv_done = sem("pv_done")
        o_low_done = sem("o_low_done")
        o_sum_done = sem("o_sum_done")
        o_hi = sem("o_hi")
        o_lo = sem("o_lo")
        gate_sig = sem("gate_sig")
        merge_part = sem("merge_part")
        merge_taken = sem("merge_taken")
        merge_sum = sem("merge_sum")
        merge_hi = sem("merge_hi")
        merge_lo = sem("merge_lo")
        block_done = sem("block_done")
        ln_part = sem("ln_part")
        ln_var = sem("ln_var")
        ln_root = sem("ln_root")
        ln_rec = sem("ln_rec")
        ln_newton = sem("ln_newton")
        ln_rstd = sem("ln_rstd")
        ln_centred = sem("ln_centred")
        ln_scaled = sem("ln_scaled")
        ln_left = sem("ln_left")
        ln_right = sem("ln_right")
        hT_done = sem("hT_done")
        hT_hi = sem("hT_hi")
        hT_ready = sem("hT_ready")
        silu_done = sem("silu_done")
        ff_done = sem("ff_done")
        a_hi = sem("a_hi")
        a_lo = sem("a_lo")
        out_landed = sem("out_landed")

        def slot(ring, n, width=D):
            start = slot_start(n)
            return ring[:, start:start + width]

        def slot_start(n):
            return 2 * D + KC // 2 * VK_W if n == N_VK[1] else n % SPL * D

        def raw_of(n):
            if n < FIRST:
                return first_raw[:, n, 0:width_of(n)]
            if n in LATE:
                return late_raw[:, n - LATE[0], :]
            return raw[:, (n % RAW) * D:(n % RAW + 1) * D]

        def landed_count(n):
            late = sum(m % RAW == n % RAW for m in LATE if m < n)
            return 16 * ((n - FIRST) // RAW + 1 - late)

        def width_of(n):
            return KC // 2 * VK_W if n in N_VK else D

        block = ctx.enter_context(nc.Block())

        @block.sync
        def _(sp):
            def load(n):
                if n < FIRST:
                    src = vk_slabs[n - N_VK[0]]
                    sp.dma_start(first_raw[:, n, 0:width_of(n)], src).then_inc(first_landed[n], 16)
                else:
                    sp.dma_start(raw[:, (n % RAW) * D:(n % RAW + 1) * D], slabs[n - 2])\
                        .then_inc(slab_landed[n % RAW], 16)

            for c in range(KC):
                sp.dma_start(x_raw[:, c, :], xT[c]).then_inc(x_landed[c], 16)
                if c < 2:
                    sp.dma_start(first_raw[:, 0, PART[c]], slabs[0][:, PART[c]]).then_inc(part_landed[c], 16)
            for q in range(2):
                sp.dma_start(first_raw[:, 1, PART[q]], slabs[1][:, PART[q]]).then_inc(part_landed[2 + q], 16)
            sp.dma_start(cs[:, :, :], rope).then_inc(cs_landed, 16)
            for n in range(2, FIRST + RAW):
                load(n)
                if n == 2:
                    sp.dma_start(cs_tok[:, :, :, :], rope_tok).then_inc(cs_tok_landed, 16)

            def load_ring(first, end):
                with sp.Fori(0, (end - first) // RAW) as i:
                    for r in range(RAW):
                        n = first + r
                        sp.wait_ge(lo_ready, i * RAW + (n - RAW + 1))
                        sp.dma_start(raw[:, (n % RAW) * D:(n % RAW + 1) * D],
                                     slabs[bass.ds(i * RAW + (n - 2), 1)].rearrange("a p n -> (a p) n"))\
                            .then_inc(slab_landed[n % RAW], 16)

            load_ring(FIRST + RAW, LATE[0])
            sp.wait_ge(merge_lo, KC)
            for n in LATE:
                sp.dma_start(late_raw[:, n - LATE[0], :], slabs[n - 2]).then_inc(late_landed[n - LATE[0]], 16)
            n = LATE[-1] + 1
            sp.wait_ge(lo_ready, LATE[0])
            sp.dma_start(raw[:, (n % RAW) * D:(n % RAW + 1) * D], slabs[n - 2]).then_inc(slab_landed[n % RAW], 16)
            load_ring(n + 1, SLABS)
            for t in range(TB):
                for q in range(2):
                    sp.wait_ge((ln_left, ln_right)[q], TB + t + 1)
                    cols = slice(512 * q, 512 * q + 512)
                    sp.dma_start(out[t * P:(t + 1) * P, cols], res[:, t, cols]).then_inc(out_landed, 16)
            sp.wait_ge(out_landed, 16 * 2 * TB)

        @block.gpsimd
        def _(pool):
            pool.memset(ident[:, :], 0.0).then_inc(consts_made, 1)
            pool.memset(ones[:, :], 1.0).then_inc(consts_made, 1)
            pool.memset(mask_b[:, :], 0.0).then_inc(consts_made, 1)
            pool.memset(stack[:, :, :], 1.0).then_inc(consts_made, 1)
            pool.wait_ge(consts_made, 4)
            pool.affine_select(out=ident[:, :], in_=ident[:, :], compare_op=ALU.not_equal, fill=1.0,
                               base=0, pattern=[[-1, P]], channel_multiplier=1).then_inc(consts_made, 1)
            pool.affine_select(out=tri[:, :], in_=ones[:, :], compare_op=ALU.is_ge, fill=0.0,
                               base=0, pattern=[[1, P]], channel_multiplier=-1).then_inc(consts_made, 1)
            pool.affine_select(out=mask_b[:, 0:P], in_=mask_b[:, 0:P], compare_op=ALU.is_gt, fill=NEG,
                               base=0, pattern=[[1, P]], channel_multiplier=-1).then_inc(consts_made, 1)
            pool.affine_select(out=mask_b[:, P:2 * P], in_=mask_b[:, P:2 * P], compare_op=ALU.is_ge, fill=NEG,
                               base=0, pattern=[[-1, P]], channel_multiplier=1).then_inc(consts_made, 1)
            pool.wait_ge(consts_made, 8)
            pool.tensor_copy(ident_b[:, :], ident[:, :]).then_inc(consts_made, 1)
            pool.memset(eps_sb[:, :], LN_EPS).then_inc(consts_made, 1)
            pool.wait_ge(x_landed[KC - 1], 16)
            pool.dma_start(sel_sb[:, :], sel).then_inc(small_landed, 16)
            pool.dma_start(bf_sb[:, :], b_forget.partition_broadcast(P)).then_inc(small_landed, 16)
            pool.dma_start(sink_sb[:, :], sinks.partition_broadcast(P)).then_inc(small_landed, 16)
            for k in range(len(N_QS)):
                pool.wait_ge(rope_rot, k + 1)
                if k == 0:
                    pool.wait_ge(cs_landed, 16)
                else:
                    pool.wait_ge(rope_sum, k)
                pool.tensor_tensor(rope3[:, :], rope2[:, :], cs[:, 1, :], ALU.mult).then_inc(rope_sin, 1)

            def slab_lo(n):
                pool.wait_ge(hi_ready, n + 1)
                pool.wait_ge(lo_ready, n)
                pool.tensor_tensor(slot(sl, n), raw_of(n), slot(sh, n).bitcast(F32), ALU.subtract)\
                    .then_inc(lo_ready, 1)

            for n in POOL_LO:
                if n < N_FF:
                    slab_lo(n)
            pool.wait_ge(pv_done, UNITS)
            pool.dma_start(res[:, :, :], x.rearrange("(t p) d -> p t d", p=P)).then_inc(res_landed, 16)
            pool.dma_start(ln1p[:, 0, :], ln1_g.partition_broadcast(P)).then_inc(res_landed, 16)
            pool.dma_start(ln1p[:, 1, :], ln1_b.partition_broadcast(P)).then_inc(res_landed, 16)

            def reciprocal_root(k):
                v, _, r, y = (rstd[:, k % 2, q:q + 1] for q in range(4))
                pool.wait_ge(ln_var, k + 1)
                if k >= 2:
                    pool.wait_ge(ln_left, k - 1)
                pool.tensor_scalar(v, mv[:, k % 2, 1:2], LN_EPS, -0.5, ALU.add, ALU.mult).then_inc(ln_newton, 1)
                pool.wait_ge(ln_rec, k + 1)
                pool.wait_ge(ln_newton, 2 * k + 1)
                pool.tensor_scalar(y, r, v, r, ALU.mult, ALU.mult).then_inc(ln_newton, 1)
                pool.wait_ge(ln_newton, 2 * k + 2)
                pool.tensor_scalar(y, y, 1.5, r, ALU.add, ALU.mult).then_inc(ln_rstd, 1)

            def right_half(k):
                r = res[:, k % TB, D // 2:D]
                b = (ln1p, ln2p)[k // TB][:, 1, D // 2:D]
                pool.wait_ge(ln_scaled, k + 1)
                pool.tensor_tensor(r, r, b, ALU.add).then_inc(ln_right, 1)

            for k in range(TB):
                reciprocal_root(k)
                if k == 0:
                    pool.wait_ge(res_landed, 48)
                if k == TB - 2:
                    slab_lo(N_FF)
                right_half(k)
                if k == TB - 2:
                    slab_lo(N_FF + 1)
                    slab_lo(N_FF + 2)
            pool.wait_ge(slab_done, N_FF)
            pool.dma_start(ln2p[:, 0, :], ln2_g.partition_broadcast(P)).then_inc(ln2_landed, 16)
            pool.dma_start(ln2p[:, 1, :], ln2_b.partition_broadcast(P)).then_inc(ln2_landed, 16)
            for k in range(TB, 2 * TB):
                reciprocal_root(k)
                if k == TB:
                    pool.wait_ge(ln2_landed, 32)
                if k != LAST_LN:
                    right_half(k)

        @block.scalar
        def _(act):
            def slab_hi(n):
                if n < FIRST:
                    act.wait_ge(first_landed[n], 16)
                elif n in LATE:
                    act.wait_ge(late_landed[n - LATE[0]], 16)
                    act.wait_ge(slab_done, n - SPL + 1)
                else:
                    act.wait_ge(slab_landed[n % RAW], landed_count(n))
                    act.wait_ge(slab_done, n - SPL + 1)
                act.activation(slot(sh, n, width_of(n)), raw_of(n), ACT.Copy).then_inc(hi_ready, 1)

            def rope_rotate(n, k):
                b = proj_bank(n)
                act.wait_ge(slab_done, n + 1)
                act.wait_ge(rope_cos, k + 1)
                if k:
                    act.wait_ge(rope_sin, k)
                else:
                    act.wait_ge(x_lo, KC)
                for q in range(4):
                    last = act.activation(rope2[32 * (q ^ 1):32 * (q ^ 1) + 32, :], ps[32 * q:32 * q + 32, b, :],
                                          ACT.Copy, scale=SCALE)
                last.then_inc(rope_rot, 1)

            def rope_split(n, k):
                act.wait_ge(rope_sum, k + 1)
                for g in range(2):
                    last = act.activation(q_s[half(g), 2 * k + g, :], rope1[k % 2][half(g), :], ACT.Copy)
                last.then_inc(rope_hi, 1)

            def keys_hi():
                act.wait_ge(kT_done, 1)
                for g in range(2):
                    for dst in range(2):
                        last = act.activation(kh_s[half(dst), g, :], ps[half(g), K_BANK, :], ACT.Copy)
                last.then_inc(kT_hi, 1)

            def take(n):
                b = proj_bank(n)
                if n == N_VK[1]:
                    act.wait_ge(slab_done, n + 1)
                    act.wait_ge(k_part, 2)
                    act.activation(v_s[:, :, :, 0:HD],
                                   ps[:, VK_BANKS, 0:KV_W].rearrange("p t (g d) -> p t g d", g=2),
                                   ACT.Copy).then_inc(vs_hi, 1)
                elif N_QF <= n < N_KF:
                    act.wait_ge(slab_done, n + 1)
                    for g in range(2):
                        last = act.activation(q_f[half(g), 2 * (n - N_QF) + g, :], ps[half(g), b, :], ACT.Copy,
                                              scale=SCALE)
                    last.then_inc(qk_hi, 1)
                elif N_KF <= n < N_V:
                    act.wait_ge(slab_done, n + 1)
                    for g in range(2):
                        for dst in range(2):
                            last = act.activation(kh_f[half(dst), 2 * (n - N_KF) + g, :], ps[half(g), b, :], ACT.Copy)
                    last.then_inc(qk_hi, 1)
                elif n == N_G - 1:
                    act.wait_ge(slab_done, n + 1)
                    for t in range(TB):
                        act.activation(v_f[:, t, :, 0:HD], ps[:, V_BANKS[t], :].rearrange("p (h d) -> p h d", d=HD),
                                       ACT.Copy).then_inc(v_hi, 1)
                elif N_G <= n < N_WO:
                    act.wait_ge(slab_done, n + 1)
                    m, w = (n - N_G) // 2, (n - N_G) % 2
                    act.activation(gates[:, m, w, :], ps[:, b, :], ACT.Copy).then_inc(gate_taken, 1)

            def exps(a):
                b = a % 2
                act.wait_ge(max_done, a + 1)
                if a >= 1:
                    act.wait_ge(probT_done, a)
                if a >= 2:
                    act.wait_ge(norm_done, a - 1)
                if a < 8:
                    j, g = unit_place(a)
                    h = j + 4 * g
                    act.activation(esink[:, b, :], nmax[:, b, :], ACT.Exp, bias=sink_sb[:, h:h + 1])
                for i, (bank, col, w, _, off) in enumerate(score_regions(a)):
                    last = act.activation(prob[:, off:off + w], ps[:, bank, col:col + w], ACT.Exp,
                                          bias=nmax[:, b, i:i + 1], accum_out=den[:, b, i:i + 1])
                last.then_inc(exp_done, 1)

            def augment(a):
                j, g = unit_place(a)
                if a == 8:
                    act.wait_ge(zeros_made, 4)
                    act.wait_ge(qk_taken, 8)
                    act.wait_ge(pv_done, 8)
                if a >= 10:
                    act.wait_ge(scores_done, a - 1)
                act.activation(q_aug[half(g), g, :], q_f[half(g), a - 8, :].bitcast(F32), ACT.Copy)
                act.activation(k_aug[half(g), g, :], kl_f[half(g), j, :].bitcast(F32), ACT.Copy)\
                    .then_inc(aug_ready, 1)

            def take_probT(a):
                act.wait_ge(probT_done, a + 1)
                if a >= 1:
                    act.wait_ge(pv_done, a)
                for k, (bank, w) in enumerate(pt_parts(a)):
                    act.activation(pth[:, 512 * k:512 * k + w], ps[:, bank, 0:w], ACT.Copy).then_inc(probT_hi, 1)

            def take_o_low(a):
                j, g = unit_place(a)
                act.wait_ge(pv_done, a + 1)
                if a >= 1:
                    act.wait_ge(o_sum_done, a)
                act.activation(o_low[half(g), :], ps[half(1), O_BANK, :], ACT.Copy).then_inc(o_low_done, 1)

            def take_o(a):
                j, g = unit_place(a)
                act.wait_ge(o_sum_done, a + 1)
                act.activation((o_s if a < 8 else o_f)[half(g), j, 0, :], o_sum[half(g), :], ACT.Copy)\
                    .then_inc(o_hi, 1)

            def rstd_root(k):
                act.wait_ge(ln_var, k + 1)
                if k == 0:
                    act.wait_ge(consts_made, 10)
                act.activation(rstd[:, k % 2, 1:2], mv[:, k % 2, 1:2], ACT.Sqrt, bias=eps_sb[:, :])\
                    .then_inc(ln_root, 1)

            def scale_right(k):
                r = res[:, k % TB, D // 2:D]
                act.wait_ge(ln_centred, k + 1)
                act.wait_ge(ln_rstd, k + 1)
                act.activation(r, r, ACT.Copy, scale=rstd[:, k % 2, 3:4]).then_inc(ln_scaled, 1)

            def h_hi(t):
                act.wait_ge(hT_done, t + 1)
                for q in range(2):
                    src = ps[:, WOUT_BANKS[t][q], :].rearrange("p (c k) -> p c k", c=4)
                    act.activation(hTh[:, 4 * q:4 * q + 4, t * P:(t + 1) * P], src, ACT.Copy)\
                        .then_inc(hT_hi, 1)

            def part_of_slab_hi(n, q):
                act.wait_ge(part_landed[2 * n + q], 16)
                act.activation(slot(sh, n)[:, PART[q]], raw_of(n)[:, PART[q]], ACT.Copy)\
                    .then_inc(hi_ready if q else part_hi, 1)

            for c in range(KC):
                act.wait_ge(x_landed[c], 16)
                act.activation(xh[:, c, :], x_raw[:, c, :], ACT.Copy).then_inc(x_hi, 1)
                if c < 2:
                    part_of_slab_hi(0, c)
            for q in range(2):
                part_of_slab_hi(1, q)
            for n in range(2, AHEAD + 1):
                slab_hi(n)

            def exp_table():
                act.activation(warm[:, :], eps_sb[:, :], ACT.Exp)

            act.wait_ge(consts_made, 10)
            exp_table()
            for n in range(1, N_WOUT + KC - WOUT_TAIL + 1):
                if n == N_QS[-2] + 1:
                    keys_hi()
                if n - 1 in N_QS and n < N_QF:
                    rope_rotate(n - 1, N_QS.index(n - 1))
                take(n - 1)
                for a in units_at(n, 2):
                    take_o_low(a)
                for a in units_at(n + 1, 0):
                    if a >= 8:
                        augment(a)
                for a in units_at(n, 1):
                    take_probT(a)
                for a in units_at(n, 0):
                    exps(a)
                if n == N_QF:
                    rope_rotate(n - 1, len(N_QS) - 1)
                for a in units_at(n, 2):
                    take_o(a)
                if N_WO <= n < N_WOUT:
                    m = n - N_WO
                    act.wait_ge(gate_taken, 2 * m + 2)
                    act.activation(gates[:, m, :, :], gates[:, m, :, :], ACT.Sigmoid).then_inc(gate_sig, 1)
                slab_hi(n + AHEAD)
                if n == N_V:
                    act.wait_ge(fg_dve, 3)
                    act.activation(fg[:, 2, :], fg[:, 1, :], ACT.Exp, scale=-1.0).then_inc(fg_act, 1)
                    act.wait_ge(fg_dve, 4)
                    act.activation(fg[:, 4, :], fg[:, 3, :], ACT.Ln).then_inc(fg_act, 1)
                    exp_table()
                for k, m in enumerate(N_QS):
                    if n == m + 1 + (k >= 2):
                        rope_split(m, k)
                if N_WO < n <= N_WOUT:
                    m = n - 1 - N_WO
                    act.wait_ge(merge_sum, m + 1)
                    act.activation(mh[:, m, :], mg[:, m % 2, :], ACT.Copy).then_inc(merge_hi, 1)
            for k in range(2):
                rstd_root(k)
                scale_right(k)
            h_hi(0)
            rstd_root(2)
            slab_hi(N_FF)
            scale_right(2)
            h_hi(1)
            slab_hi(N_FF + 1)
            slab_hi(N_FF + 2)
            rstd_root(3)
            h_hi(2)
            scale_right(3)
            slab_hi(N_FF + 3)
            h_hi(3)

            def silu(f):
                act.wait_ge(slab_done, N_FF + 2 * f + 1)
                act.activation(sg[:, f % 2, :], ps[:, FF_BANKS[f % 2][0], :], ACT.Silu).then_inc(silu_done, 1)

            for r in range(4):
                if r % 2:
                    silu(r // 2)
                slab_hi(N_FF + r + 4)
            for k in range(2):
                act.wait_ge(ff_done, k + 1)
                act.activation(ah[:, k, :], ffT[:, k, :], ACT.Copy).then_inc(a_hi, 1)

            with act.Fori(1, FT // 2) as i:
                for r in range(4):
                    m = N_FF + r + AHEAD + 1
                    if r % 2:
                        fi = r // 2
                        act.wait_ge(slab_done, i * 4 + (N_FF + r))
                        act.wait_ge(ff_done, i * 2 + (fi - 1))
                        act.activation(sg[:, fi, :], ps[:, FF_BANKS[fi][0], :], ACT.Silu).then_inc(silu_done, 1)
                    act.wait_ge(slab_landed[m % RAW], i * (16 * 4 // RAW) + landed_count(m))
                    act.wait_ge(slab_done, i * 4 + (m - SPL + 1))
                    act.activation(slot(sh, m), raw_of(m), ACT.Copy).then_inc(hi_ready, 1)

            def down_step(i, r, slab, split):
                m = N_DN + r + AHEAD + 1
                if split:
                    act.wait_ge(slab_done, i * 4 + (N_DN + r - 1))
                    act.wait_ge(ff_done, i * 4 + (r + 3))
                    s = (r + 2) % SPL
                    act.activation(ah[:, s:s + 1, :], ffT[:, bass.ds(i * 4 + (r + 2), 1), :], ACT.Copy)\
                        .then_inc(a_hi, 1)
                if slab:
                    act.wait_ge(slab_landed[m % RAW], i * (16 * 4 // RAW) + landed_count(m))
                    act.wait_ge(slab_done, i * 4 + (m - SPL + 1))
                    act.activation(slot(sh, m), raw_of(m), ACT.Copy).then_inc(hi_ready, 1)

            with act.Fori(0, 4) as i:
                for r in range(4):
                    down_step(i, r, True, True)
            down_step(4, 0, True, True)
            down_step(4, 1, False, True)
            down_step(4, 2, False, True)
            down_step(4, 1, True, False)
            down_step(4, 3, False, True)
            for t in range(TB):
                rstd_root(TB + t)
                if TB + t != LAST_LN:
                    scale_right(TB + t)

        @block.vector
        def _(dve):
            def slab_lo(n):
                dve.wait_ge(hi_ready, n + 1)
                if n - 1 in POOL_LO:
                    dve.wait_ge(lo_ready, n)
                w = width_of(n)
                dve.tensor_tensor(slot(sl, n, w), raw_of(n), slot(sh, n, w).bitcast(F32),
                                  ALU.subtract).then_inc(lo_ready, 1)

            def low(dst, src, hi):
                return dve.tensor_tensor(dst, src, hi.bitcast(F32), ALU.subtract)

            def rope_cosine(n, k):
                dve.wait_ge(slab_done, n + 1)
                if k == 0:
                    dve.wait_ge(cs_landed, 16)
                if k >= 2:
                    dve.wait_ge(rope_done, k - 1)
                dve.scalar_tensor_tensor(out=rope1[k % 2][:, :], in0=ps[:, proj_bank(n), :],
                                         scalar=SCALE, in1=cs[:, 0, :],
                                         op0=ALU.mult, op1=ALU.mult).then_inc(rope_cos, 1)

            def rope_add(k):
                dve.wait_ge(rope_sin, k + 1)
                dve.wait_ge(rope_cos, k + 1)
                dve.tensor_tensor(rope1[k % 2][:, :], rope1[k % 2][:, :], rope3[:, :], ALU.add).then_inc(rope_sum, 1)

            def rope_low(n, k):
                dve.wait_ge(rope_sum, k + 1)
                dve.wait_ge(rope_hi, k + 1)
                for g in range(2):
                    h = 2 * k + g
                    last = low(q_s[half(1 - g), h, :], rope1[k % 2][half(g), :], q_s[half(g), h, :])
                last.then_inc(rope_done, 1)

            def rotate_keys():
                dve.wait_ge(cs_tok_landed, 16)
                k = ps[:, VK_BANKS, KV_W:2 * KV_W].rearrange("p t (g h d) -> p t g h d", g=2, h=2)
                cos, sin = (cs_tok[:, :, w, :].unsqueeze(2).broadcast_to([P, TB, 2, HD // 2]) for w in range(2))
                for h in range(2):
                    dve.tensor_tensor(k_rot[:, :, :, h, :], k[:, :, :, h, :], cos, ALU.mult)
                for h in range(2):
                    dve.tensor_tensor(k_sin[:, :, :, h, :], k[:, :, :, 1 - h, :], sin, ALU.mult).then_inc(k_part, 1)
                dve.wait_ge(k_part, 2)
                for h in range(2):
                    dve.tensor_tensor(k_rot[:, :, :, h, :], k_rot[:, :, :, h, :], k_sin[:, :, :, h, :],
                                      ALU.add if h else ALU.subtract).then_inc(k_rotated, 1)

            def keys_low():
                dve.wait_ge(kT_hi, 1)
                for g in range(2):
                    last = low(kl_s[half(g), :], ps[half(g), K_BANK, :], kh_s[half(g), g, :])
                last.then_inc(ks_taken, 1)

            def take(n):
                b = proj_bank(n)
                if n == N_VK[1]:
                    dve.wait_ge(vs_hi, 1)
                    low(v_s[:, :, :, HD:2 * HD], ps[:, VK_BANKS, 0:KV_W].rearrange("p t (g d) -> p t g d", g=2),
                        v_s[:, :, :, 0:HD]).then_inc(vs_taken, 1)
                elif N_QF <= n < N_KF:
                    dve.wait_ge(qk_hi, n - N_QF + 1)
                    for g in range(2):
                        h = 2 * (n - N_QF) + g
                        last = dve.scalar_tensor_tensor(
                            out=q_f[half(1 - g), h, :], in0=ps[half(g), b, :], scalar=SCALE,
                            in1=q_f[half(g), h, :].bitcast(F32), op0=ALU.mult, op1=ALU.subtract)
                    last.then_inc(qk_taken, 1)
                elif N_KF <= n < N_V:
                    dve.wait_ge(qk_hi, n - N_QF + 1)
                    for g in range(2):
                        h = 2 * (n - N_KF) + g
                        last = low(kl_f[half(g), n - N_KF, :], ps[half(g), b, :], kh_f[half(g), h, :])
                    last.then_inc(qk_taken, 1)
                elif n == N_G - 1:
                    for t in range(TB):
                        dve.wait_ge(v_hi, t + 1)
                        low(v_f[:, t, :, HD:2 * HD], ps[:, V_BANKS[t], :].rearrange("p (h d) -> p h d", d=HD),
                            v_f[:, t, :, 0:HD]).then_inc(v_taken, 1)

            fgn = [0]

            def fg_step(ins):
                fgn[0] += 1
                ins.then_inc(fg_dve, 1)
                dve.wait_ge(fg_dve, fgn[0])

            def forget_logits():
                dve.wait_ge(slab_done, N_VK[1] + 1)
                dve.wait_ge(small_landed, 48)
                logit = ps[:, VK_BANKS, 2 * KV_W:VK_W]
                bf = bf_sb[:, :].unsqueeze(1).broadcast_to([P, TB, HEADS])
                fg_step(dve.tensor_tensor(fg[:, 0, :].rearrange("p (t h) -> p t h", t=TB), logit, bf, ALU.add))

            def forget_gate():
                z, az, e, u, lnu, um, d, ru, mn, lf = (fg[:, k, :] for k in range(10))
                fg_step(dve.tensor_scalar(az, z, -1.0, None, ALU.mult))
                fg_step(dve.tensor_tensor(az, z, az, ALU.max))
                dve.wait_ge(fg_act, 1)
                fg_step(dve.tensor_scalar(u, e, 1.0, None, ALU.add))
                fg_step(dve.tensor_scalar(um, u, -1.0, None, ALU.add))
                fg_step(dve.tensor_tensor(d, e, um, ALU.subtract))
                fg_step(dve.reciprocal(ru, u))
                fg_step(dve.tensor_tensor(d, d, ru, ALU.mult))
                fg_step(dve.tensor_scalar(mn, z, 0.0, None, ALU.min))
                fg_step(dve.tensor_tensor(mn, mn, d, ALU.subtract))
                dve.wait_ge(fg_act, 2)
                fg_step(dve.tensor_tensor(lf, mn, lnu, ALU.subtract))
                before, w = fg[:, 1, :], HEADS
                fg_step(dve.tensor_copy(before[:, w:2 * w], lf[:, 0:w]))
                for t in range(2, TB):
                    fg_step(dve.tensor_tensor(before[:, t * w:(t + 1) * w], before[:, (t - 1) * w:t * w],
                                              lf[:, (t - 1) * w:t * w], ALU.add))

            def bias_stacks():
                dve.wait_ge(cum_done, 1)
                c_sb, c_lo = fg[:, 0, :], fg[:, 1, :]
                fg_step(dve.tensor_copy(c_sb, ps[:, C_BANK, 0:TB * HEADS]))
                fg_step(dve.tensor_copy(c_hi[:, :], c_sb))
                fg_step(dve.tensor_tensor(c_lo, c_sb, c_hi[:, :].bitcast(F32), ALU.subtract))
                dve.wait_ge(consts_made, 4)
                th = lambda ap: ap.rearrange("p (t h) -> p t h", t=TB)
                fg_step(dve.tensor_scalar(stack[:, :, 0:8], th(c_hi[:, :].bitcast(F32)), -1.0, None, ALU.mult))
                fg_step(dve.tensor_scalar(stack[:, :, 8:16], th(c_lo), -1.0, None, ALU.mult))
                fg_step(dve.tensor_copy(stack[:, :, 48:56], th(c_hi[:, :].bitcast(F32))))
                fg_step(dve.tensor_copy(stack[:, :, 56:64], th(c_lo)))

            def take_stacks():
                dve.wait_ge(stackT_done, 1)
                dve.wait_ge(pv_done, 8)
                for t in (q_aug, k_aug):
                    for g in range(2):
                        dve.memset(t[zero_rows(g), g, :].bitcast(F32), 0.0).then_inc(zeros_made, 1)
                for g in range(2):
                    dve.tensor_copy(k_aug[bias_rows(g), g, :], ps[0:32, C_BANK, :]).then_inc(bias_ready, 1)
                dve.tensor_copy(bias_l32[:, :], ps[32:64, C_BANK, :]).then_inc(bias_ready, 1)

            def head_bias(h):
                dve.wait_ge(bias_ready, 3)
                if h >= 2:
                    dve.wait_ge(scores_done, 8 + h - 1)
                dve.tensor_scalar(q_aug[bias_rows(h % 2), h % 2, :], bias_l32[:, :], sel_sb[:, h:h + 1],
                                  None, ALU.mult).then_inc(bias_l_ready, 1)

            def maxima(a):
                b = a % 2
                dve.wait_ge(scores_done, a + 1)
                if a >= 2:
                    dve.wait_ge(exp_done, a - 1)
                j, g = unit_place(a)
                for i, (bank, col, w, _, _) in enumerate(score_regions(a)):
                    s = ps[:, bank, col:col + w]
                    if a < 8:
                        dve.tensor_reduce(smax[:, b, i:i + 1], s, AX_X, ALU.max).then_inc(max_part, 1)
                    else:
                        last = dve.tensor_reduce(nmax[:, b, i:i + 1], s, AX_X, ALU.max, negate=True)
                if a < 8:
                    h = j + 4 * g
                    dve.wait_ge(max_part, 4 * (a + 1))
                    last = dve.tensor_scalar(nmax[:, b, :], smax[:, b, :], sink_sb[:, h:h + 1], -1.0,
                                             ALU.max, ALU.mult)
                last.then_inc(max_done, 1)

            def normalise(a):
                b = a % 2
                dve.wait_ge(exp_done, a + 1)
                if a < 8:
                    dve.tensor_tensor(den[:, b, :], den[:, b, :], esink[:, b, :], ALU.add).then_inc(den_part, 1)
                    dve.wait_ge(den_part, a + 1)
                dve.reciprocal(rden[:, b, :], den[:, b, :]).then_inc(rden_done, 1)
                dve.wait_ge(rden_done, a + 1)
                for i, (_, _, w, _, off) in enumerate(score_regions(a)):
                    last = dve.tensor_scalar(prob[:, off:off + w], prob[:, off:off + w],
                                             rden[:, b, i:i + 1], None, ALU.mult)
                last.then_inc(norm_done, 1)

            def take_probT(a):
                for k, (bank, w) in enumerate(pt_parts(a)):
                    dve.wait_ge(probT_hi, probT_parts_before(a) + k + 1)
                    last = low(ptl[:, 512 * k:512 * k + w], ps[:, bank, 0:w], pth[:, 512 * k:512 * k + w])
                last.then_inc(probT_taken, 1)

            def sum_o(a):
                j, g = unit_place(a)
                dve.wait_ge(o_low_done, a + 1)
                if a >= 1:
                    dve.wait_ge(o_lo, a)
                dve.tensor_tensor(o_sum[half(g), :], ps[half(0), O_BANK, :], o_low[half(g), :], ALU.add)\
                    .then_inc(o_sum_done, 1)

            def take_o(a):
                j, g = unit_place(a)
                dst = o_s if a < 8 else o_f
                dve.wait_ge(o_hi, a + 1)
                dve.wait_ge(o_sum_done, a + 1)
                low(dst[half(g), j, 1, :], o_sum[half(g), :], dst[half(g), j, 0, :]).then_inc(o_lo, 1)

            def merge(m):
                b = 2 + 2 * (m % 2)
                dve.wait_ge(slab_done, N_WO + m + 1)
                dve.wait_ge(gate_sig, m + 1)
                if m >= 1:
                    dve.wait_ge(merge_sum, m)
                dve.tensor_tensor(mt1[:, :], gates[:, m, 0, :], ps[:, b, :], ALU.mult).then_inc(merge_part, 1)
                dve.tensor_tensor(mt2[:, :], gates[:, m, 1, :], ps[:, b + 1, :], ALU.mult).then_inc(merge_taken, 1)
                dve.wait_ge(merge_part, m + 1)
                dve.wait_ge(merge_taken, m + 1)
                if m >= 2:
                    dve.wait_ge(merge_hi, m - 1)
                dve.tensor_tensor(mg[:, m % 2, :], mt1[:, :], mt2[:, :], ALU.add).then_inc(merge_sum, 1)

            def merge_low(m):
                dve.wait_ge(merge_hi, m + 1)
                dve.tensor_tensor(ml[:, m, :], mg[:, m % 2, :], mh[:, m, :].bitcast(F32), ALU.subtract)\
                    .then_inc(merge_lo, 1)

            steps = [0]

            def signal(ins):
                ins.then_inc(ln_part, 1)
                steps[0] += 1
                return steps[0]

            def columns(q):
                return slice(512 * q, 512 * q + 512)

            def residual(k, q):
                t, banks = k % TB, (WOUT_BANKS, DN_BANKS)[k // TB][k % TB]
                if q == 0 and k == 0:
                    dve.wait_ge(res_landed, 48)
                if q == 0 and k >= TB:
                    dve.wait_ge(ln_left, t + 1)
                    dve.wait_ge(ln_right, t + 1)
                if q == 0 and k >= 2:
                    dve.wait_ge(ln_right, k - 1)
                if k == TB - 1:
                    dve.wait_ge(slab_done, N_FF)
                else:
                    dve.wait_ge(block_done, 2 * (k - (k >= TB)) + q + 1)
                r = res[:, t, columns(q)]
                return signal(dve.scalar_tensor_tensor(out=r, in0=r, scalar=ALPHA, in1=ps[:, banks[q], :],
                                                       op0=ALU.mult, op1=ALU.add))

            def statistics(k, q, after):
                dve.wait_ge(ln_part, after)
                return signal(dve.bn_stats(stats[:, k % 2, 6 * q:6 * q + 6], res[:, k % TB, columns(q)]))

            def centre(k, after):
                s, gamma = k % 2, (ln1p, ln2p)[k // TB]
                if k == TB:
                    dve.wait_ge(ln2_landed, 32)
                dve.wait_ge(ln_part, after)
                dve.bn_aggr(mv[:, s, :], stats[:, s, :]).then_inc(ln_var, 1)
                dve.wait_ge(ln_var, k + 1)
                cuts = (0, 256, 512, D) if k == LAST_LN else (0, 512, D)
                for i, (lo, hi) in enumerate(zip(cuts, cuts[1:])):
                    r = res[:, k % TB, lo:hi]
                    ins = dve.scalar_tensor_tensor(out=r, in0=r, scalar=mv[:, s, 0:1], in1=gamma[:, 0, lo:hi],
                                                   op0=ALU.subtract, op1=ALU.mult)
                    if hi == D:
                        ins.then_inc(ln_centred, 1)
                    else:
                        left = signal(ins)
                    if i == 0:
                        dve.wait_ge(ln_root, k + 1)
                        dve.reciprocal(rstd[:, s, 2:3], rstd[:, s, 1:2]).then_inc(ln_rec, 1)
                return left

            def scale(k, left):
                beta = (ln1p, ln2p)[k // TB]
                dve.wait_ge(ln_part, left)
                dve.wait_ge(ln_rstd, k + 1)
                for q in range(2 if k == LAST_LN else 1):
                    if q:
                        dve.wait_ge(ln_centred, k + 1)
                    r = res[:, k % TB, columns(q)]
                    dve.scalar_tensor_tensor(out=r, in0=r, scalar=rstd[:, k % 2, 3:4], in1=beta[:, 1, columns(q)],
                                             op0=ALU.mult, op1=ALU.add).then_inc(ln_right if q else ln_left, 1)

            def layer_norm(k):
                first, second = residual(k, 0), residual(k, 1)
                statistics(k, 0, first)
                scale(k, centre(k, statistics(k, 1, second)))

            def last_two():
                k = LAST_LN - 1
                first, second = residual(k, 0), residual(k, 1)
                statistics(k, 0, first)
                left = centre(k, statistics(k, 1, second))
                first = residual(LAST_LN, 0)
                scale(k, left)
                statistics(LAST_LN, 0, first)
                scale(LAST_LN, centre(LAST_LN, statistics(LAST_LN, 1, residual(LAST_LN, 1))))

            def h_lo(t):
                tok = slice(t * P, (t + 1) * P)
                for q in range(2):
                    dve.wait_ge(hT_hi, 2 * t + q + 1)
                    src = ps[:, WOUT_BANKS[t][q], :].rearrange("p (c q) -> p c q", c=4)
                    last = low(hTl[:, 4 * q:4 * q + 4, tok], src, hTh[:, 4 * q:4 * q + 4, tok])
                last.then_inc(hT_ready, 1)

            def part_of_slab_lo(n, q):
                dve.wait_ge(hi_ready if q else part_hi, n + 1)
                low(slot(sl, n)[:, PART[q]], raw_of(n)[:, PART[q]], slot(sh, n)[:, PART[q]])\
                    .then_inc(lo_ready if q else part_lo, 1)

            for c in range(KC):
                dve.wait_ge(x_hi, c + 1)
                dve.tensor_tensor(xl[:, c, :], x_raw[:, c, :], xh[:, c, :].bitcast(F32), ALU.subtract)\
                    .then_inc(x_lo, 1)
                if c < 2:
                    part_of_slab_lo(0, c)
            for q in range(2):
                part_of_slab_lo(1, q)
            for n in range(2, AHEAD + 1):
                slab_lo(n)
            def rope_rest(n):
                for k, m in enumerate(N_QS):
                    if n == m + 2 + (k >= 2):
                        rope_low(m, k)
                    if k >= 2 and n == m + 2:
                        rope_add(k)

            for n in range(1, N_WOUT + KC - WOUT_TAIL + 1):
                for a in units_at(n, 0):
                    maxima(a)
                if n - 1 in N_QS:
                    rope_cosine(n - 1, N_QS.index(n - 1))
                if n == N_QS[-2] + 1:
                    keys_low()
                if n < N_QF:
                    rope_rest(n)
                if n == N_VK[1] + 1:
                    forget_logits()
                    rotate_keys()
                    slab_lo(n - 1 + AHEAD)
                take(n - 1)
                for a in units_at(n, 2):
                    sum_o(a)
                if n == N_CUM + 1:
                    take_stacks()
                for a in units_at(n + 1, 0):
                    if a >= 8:
                        head_bias(a - 8)
                for a in units_at(n, 1):
                    take_probT(a)
                if n >= N_QF:
                    rope_rest(n)
                if n == N_CUM:
                    bias_stacks()
                for a in units_at(n, 0):
                    normalise(a)
                for a in units_at(n, 2):
                    take_o(a)
                if N_WO < n <= N_WOUT:
                    merge(n - 1 - N_WO)
                if n - 1 in N_QS[:2]:
                    rope_add(N_QS.index(n - 1))
                if n + AHEAD not in POOL_LO and n != N_VK[1]:
                    slab_lo(n + AHEAD)
                if n == N_V:
                    forget_gate()
                if N_WO < n <= N_WOUT:
                    merge_low(n - 1 - N_WO)
            for t in range(3):
                layer_norm(t)
            h_lo(0)
            h_lo(1)
            layer_norm(3)
            h_lo(2)
            slab_lo(N_FF + 3)
            h_lo(3)

            def hidden(f):
                dve.wait_ge(silu_done, f + 1)
                dve.wait_ge(slab_done, N_FF + 2 * f + 2)
                dve.tensor_tensor(ffT[:, f, :], sg[:, f, :], ps[:, FF_BANKS[f][1], :], ALU.mult).then_inc(ff_done, 1)

            for r in range(4):
                if r % 2:
                    hidden(r // 2)
                slab_lo(N_FF + r + 4)
            for k in range(2):
                dve.wait_ge(a_hi, k + 1)
                low(al[:, k, :], ffT[:, k, :], ah[:, k, :]).then_inc(a_lo, 1)
            with dve.Fori(1, FT // 2) as i:
                for r in range(4):
                    m = N_FF + r + AHEAD + 1
                    if r % 2:
                        fi = r // 2
                        dve.wait_ge(silu_done, i * 2 + (fi + 1))
                        dve.wait_ge(slab_done, i * 4 + (N_FF + r + 1))
                        dve.tensor_tensor(ffT[:, bass.ds(i * 2 + fi, 1), :], sg[:, fi:fi + 1, :],
                                          ps[:, FF_BANKS[fi][1]:FF_BANKS[fi][1] + 1, :], ALU.mult)\
                            .then_inc(ff_done, 1)
                    dve.wait_ge(hi_ready, i * 4 + (m + 1))
                    low(slot(sl, m), raw_of(m), slot(sh, m)).then_inc(lo_ready, 1)

            def down_step(i, r, slab, split):
                m = N_DN + r + AHEAD + 1
                if split:
                    dve.wait_ge(a_hi, i * 4 + (r + 3))
                    s = (r + 2) % SPL
                    low(al[:, s:s + 1, :], ffT[:, bass.ds(i * 4 + (r + 2), 1), :], ah[:, s:s + 1, :])\
                        .then_inc(a_lo, 1)
                if slab:
                    dve.wait_ge(hi_ready, i * 4 + (m + 1))
                    low(slot(sl, m), raw_of(m), slot(sh, m)).then_inc(lo_ready, 1)

            with dve.Fori(0, 4) as i:
                for r in range(4):
                    down_step(i, r, True, True)
            down_step(4, 0, True, True)
            down_step(4, 1, False, True)
            down_step(4, 2, False, True)
            down_step(4, 1, True, False)
            down_step(4, 3, False, True)
            layer_norm(TB)
            layer_norm(TB + 1)
            last_two()

        @block.tensor
        def _(pe):
            def mm3(dst, lh, ll, rh, rl, start, stop):
                pe.matmul(dst, lh, rh, start=start, stop=False)
                pe.matmul(dst, ll, rh, start=False, stop=False)
                return pe.matmul(dst, lh, rl, start=False, stop=stop)

            def cut(n, a, b):
                s = slot_start(n)
                return sh[:, s + a:s + b], sl[:, s + a:s + b]

            def scores(a):
                u = a % 8
                j, g = unit_place(a)
                regions = score_regions(a)
                q, kh = (q_s[:, u, :], kh_s[:, g, :]) if a < 8 else (q_f[:, u, :], kh_f[:, u, :])
                qh, kl = (q[half(g), :], kl_s[half(g), :]) if a < 8 else (q_aug[:, g, :], k_aug[:, g, :])
                if a == 0:
                    pe.wait_ge(vs_taken, 1)
                    pe.wait_ge(ks_taken, 1)
                    pe.wait_ge(consts_made, 9)
                elif a == 8:
                    pe.wait_ge(v_taken, TB)
                    pe.wait_ge(qk_taken, 8)
                else:
                    pe.wait_ge(exp_done, a)
                if a < 8:
                    pe.wait_ge(rope_done, 1 + j)
                else:
                    pe.wait_ge(bias_l_ready, u + 1)
                    pe.wait_ge(aug_ready, u + 1)
                seen = set()
                for i, (bank, col, w, k0, _) in enumerate(regions):
                    pe.matmul(ps[:, bank, col:col + w], q[:, i * P:(i + 1) * P], kh[:, k0 * P:k0 * P + w],
                              start=bank not in seen, stop=False, skip_group_check=True)
                    seen.add(bank)
                for i, (bank, col, w, k0, _) in enumerate(regions):
                    pe.matmul(ps[:, bank, col:col + w], qh[:, i * P:(i + 1) * P], kl[:, k0 * P:k0 * P + w],
                              start=False, stop=False, skip_group_check=True)
                for i, (bank, col, w, _, _) in enumerate(regions):
                    mw = min(w, 2 * P) if a < 8 else P
                    last = pe.matmul(ps[:, bank, col + w - mw:col + w], ident_b[:, :], mask_b[:, 2 * P - mw:2 * P],
                                     start=False, stop=True, skip_group_check=True)
                last.then_inc(scores_done, 1)

            def turn_keys():
                pe.wait_ge(k_rotated, 2)
                pe.wait_ge(rope_rot, 1)
                pe.wait_ge(consts_made, 9)
                for t in range(TB):
                    last = pe.transpose(ps[:, K_BANK, t * P:(t + 1) * P],
                                        k_rot[:, t, :, :, :].rearrange("p g h d -> p (g h d)"), ident[:, :])
                last.then_inc(kT_done, 1)

            def transposes(a):
                pe.wait_ge(norm_done, a + 1)
                if a == 0:
                    pe.wait_ge(rope_rot, 4)
                if a >= 1:
                    pe.wait_ge(probT_taken, a)
                keys = key_regions(a)
                for i, (_, _, w, _, off) in enumerate(score_regions(a)):
                    k0 = i + 1 - w // P
                    for kb in range(k0, i + 1):
                        col = keys[kb][0] + (i - kb) * P
                        last = pe.transpose(ps[:, 5 + col // 512, col % 512:col % 512 + P],
                                            prob[:, off + (kb - k0) * P:off + (kb - k0 + 1) * P], ident[:, :])
                last.then_inc(probT_done, 1)

            def values(a):
                _, g = unit_place(a)
                pe.wait_ge(probT_taken, a + 1)
                if a >= 1:
                    pe.wait_ge(o_sum_done, a)
                for kb, (col, w) in enumerate(key_regions(a)):
                    v = v_s[:, kb, g, :] if a < 8 else v_f[:, kb, a - 8, :]
                    for part in (pth, ptl):
                        last = pe.matmul(ps[:, O_BANK, kb * P:kb * P + w], v, part[:, col:col + w],
                                         start=(kb == 0 and part is pth), stop=(kb == TB - 1 and part is ptl),
                                         skip_group_check=True)
                last.then_inc(pv_done, 1)

            def cumulative():
                pe.wait_ge(fg_dve, 14)
                pe.wait_ge(qk_taken, 8)
                pe.matmul(ps[:, C_BANK, 0:TB * HEADS], tri[:, :], fg[:, 9, :], start=True, stop=False,
                          skip_group_check=True)
                pe.matmul(ps[:, C_BANK, HEADS:TB * HEADS], ones[:, :], fg[:, 1, HEADS:TB * HEADS],
                          start=False, stop=True, skip_group_check=True).then_inc(cum_done, 1)

            def stacks():
                pe.wait_ge(fg_dve, 21)
                for t in range(TB):
                    last = pe.transpose(ps[0:64, C_BANK, t * P:(t + 1) * P], stack[:, t, :], ident[:, :])
                last.then_inc(stackT_done, 1)

            def bank_free(n):
                if n == 6:
                    pe.wait_ge(ks_taken, 1)
                elif n == 7:
                    pe.wait_ge(rope_rot, 2)
                elif 8 <= n < N_V:
                    pe.wait_ge(qk_taken, n - 7)
                elif n == N_V:
                    pe.wait_ge(exp_done, 8)
                    pe.wait_ge(qk_taken, 7)
                elif n == N_G:
                    pe.wait_ge(bias_ready, 3)
                elif N_G < n < 27:
                    pe.wait_ge(gate_taken, n - N_G)
                elif n in (27, 28):
                    pe.wait_ge(exp_done, UNITS)
                elif n == 30:
                    pe.wait_ge(o_sum_done, UNITS)
                elif 28 < n < N_WO:
                    pe.wait_ge(gate_taken, n - N_G - 1)
                elif n in (N_WO, N_WO + 1):
                    pe.wait_ge(exp_done, UNITS)
                    pe.wait_ge(probT_taken, UNITS)
                elif N_WO + 2 <= n < N_WOUT:
                    pe.wait_ge(merge_taken, n - N_WO - 1)

            def slab(n, between):
                if n >= 2:
                    pe.wait_ge(lo_ready, n + 1)
                bank_free(n)
                b = proj_bank(n)
                if n in N_VK:
                    for t in range(TB):
                        dst = ps[:, VK_BANKS.start + t, 0:VK_W]
                        for i in range(KC // 2):
                            c = KC // 2 * (n - N_VK[0]) + i
                            tok = slice(t * P, (t + 1) * P)
                            last = mm3(dst, xh[:, c, tok], xl[:, c, tok], *cut(n, i * VK_W, (i + 1) * VK_W),
                                       start=(c == 0), stop=(c == KC - 1))
                elif N_V <= n < N_G:
                    for t in range(TB):
                        if t == 1:
                            between()
                        for i in range(2):
                            c = 2 * (n - N_V) + i
                            tok = slice(t * P, (t + 1) * P)
                            last = mm3(ps[:, V_BANKS[t], :], xh[:, c, tok], xl[:, c, tok],
                                       *cut(n, i * FOX_W, (i + 1) * FOX_W), start=(c == 0), stop=(c == KC - 1))
                elif n < N_WO:
                    for c in range(KC):
                        if n < 2 and c == 0:
                            pe.wait_ge(part_lo, n + 1)
                        if n < 2 and c == KC // 2:
                            pe.wait_ge(lo_ready, n + 1)
                        if n == 0:
                            pe.wait_ge(x_lo, c + 1)
                        if c == 2:
                            between()
                        last = mm3(ps[:, b, :], *cut(n, c * P, (c + 1) * P), xh[:, c, :], xl[:, c, :],
                                   start=(c == 0), stop=(c == KC - 1))
                else:
                    pe.wait_ge(o_lo, UNITS)
                    b = 2 + 2 * (n % 2)
                    for c in range(8):
                        o = o_f[:, c, :, :] if c < 4 else o_s[:, c - 4, :, :]
                        last = mm3(ps[:, b + c // 4, :], *cut(n, c * P, (c + 1) * P), o[:, 0, :], o[:, 1, :],
                                   start=(c % 4 == 0), stop=(c % 4 == 3))
                last.then_inc(slab_done, 1)

            def rows(n, c, lhs, bank, q, t, start, stop):
                return mm3(ps[:, bank, :], *lhs(c, t), *cut(n, 512 * q, 512 * q + 512), start=start, stop=stop)

            def merged(c, t):
                return mh[:, c, t * P:(t + 1) * P], ml[:, c, t * P:(t + 1) * P]

            def turn(n):
                if n == N_QS[-1]:
                    turn_keys()
                for a in units_at(n, 1):
                    transposes(a)

            pe.wait_ge(consts_made, 4)
            for _ in range(WARM_UP):
                pe.matmul(ps[:, VK_BANKS.start, 0:P], ones[:, :], ones[:, :], start=True, stop=True)
            for n in range(N_WOUT):
                for a in units_at(n, 0):
                    scores(a)
                for a in units_at(n, 2):
                    values(a)
                if n == N_CUM:
                    cumulative()
                if n == N_CUM + 1:
                    stacks()
                slab(n, lambda: turn(n))

            def by_blocks(n0, first, count, lhs, banks, slab_wait, hook, signal_slabs):
                end = first + count - 1
                for t in range(TB):
                    slabwise = t == 0 or (signal_slabs and t == TB - 1)
                    order = [(c, q) for c in range(first, end + 1) for q in range(2)]
                    if not slabwise:
                        order.sort(key=lambda cq: (cq[1], cq[0]))
                    for c, q in order:
                        if t == 0 and q == 0:
                            slab_wait(c)
                        if q == 0:
                            hook(t, c)
                        last = rows(n0 + c, c, lhs, banks[t][q], q, t, start=False, stop=(c == end))
                        if signal_slabs and t == TB - 1:
                            if q == 1:
                                last.then_inc(slab_done, 1)
                        elif c == end:
                            last.then_inc(block_done, 1)

            for c in range(KC - WOUT_TAIL):
                n = N_WOUT + c
                pe.wait_ge(lo_ready, n + 1)
                pe.wait_ge(merge_lo, c + 1)
                for t in range(TB):
                    if c == 0 and t == 1:
                        pe.wait_ge(gate_taken, 16)
                    if c == 0 and t >= 2:
                        pe.wait_ge(merge_taken, 5 + t)
                    for q in range(2):
                        last = rows(n, c, merged, WOUT_BANKS[t][q], q, t, start=(c == 0), stop=False)
                last.then_inc(slab_done, 1)

            def turn_h(t):
                pe.wait_ge(ln_left, t + 1)
                pe.wait_ge(ln_right, t + 1)
                for c in range(KC):
                    last = pe.transpose(ps[:, WOUT_BANKS[t][c // 4], (c % 4) * P:(c % 4 + 1) * P],
                                        res[:, t, c * P:(c + 1) * P], ident[:, :])
                last.then_inc(hT_done, 1)

            def wait_wout(c):
                pe.wait_ge(lo_ready, N_WOUT + c + 1)
                pe.wait_ge(merge_lo, c + 1)

            def between_wout(t, c):
                if t == TB - 1 and c == KC - WOUT_TAIL:
                    turn_h(0)
                if t == TB - 1 and c == KC - 2:
                    turn_h(1)

            by_blocks(N_WOUT, KC - WOUT_TAIL, WOUT_TAIL, merged, WOUT_BANKS, wait_wout, between_wout, True)

            def ff_slab(n, f, w, tokens, signal):
                for c in range(KC):
                    last = mm3(ps[:, FF_BANKS[f % 2][w], tokens], *cut(n, c * P, (c + 1) * P),
                               hTh[:, c, tokens], hTl[:, c, tokens], start=(c == 0), stop=(c == KC - 1))
                if signal:
                    last.then_inc(slab_done, 1)

            pe.wait_ge(hT_ready, 2)
            for r in range(4):
                pe.wait_ge(lo_ready, N_FF + r + 1)
                ff_slab(N_FF + r, r // 2, r % 2, slice(0, 2 * P), False)
                if r == 0:
                    turn_h(2)
                elif r == 2:
                    turn_h(3)
            pe.wait_ge(hT_ready, 4)
            for r in range(4):
                ff_slab(N_FF + r, r // 2, r % 2, slice(2 * P, SEQ), True)
            with pe.Fori(1, FT // 2) as i:
                for r in range(4):
                    n = N_FF + r
                    pe.wait_ge(lo_ready, i * 4 + (n + 1))
                    if r % 2 == 0:
                        pe.wait_ge(ff_done, i * 2 + (r // 2 - 1))
                    ff_slab(n, r // 2, r % 2, slice(0, SEQ), True)

            def hidden(c, t):
                s = c % SPL
                return ah[:, s, t * P:(t + 1) * P], al[:, s, t * P:(t + 1) * P]

            def down(i, r, peel):
                n = N_DN + r
                pe.wait_ge(lo_ready, i * 4 + (n + 1))
                pe.wait_ge(a_lo, i * 4 + (r + 1))
                for t in range(TB):
                    if peel and t >= 2:
                        pe.wait_ge(ff_done, FT + t - 3)
                    for q in range(2):
                        last = rows(n, r, hidden, DN_BANKS[t][q], q, t, start=peel, stop=False)
                last.then_inc(slab_done, 1)

            for r in range(4):
                down(0, r, r == 0)
            with pe.Fori(1, 4) as i:
                for r in range(4):
                    down(i, r, False)
            for r in range(FT - DN_TAIL - 16):
                down(4, r, False)

            def wait_down(c):
                pe.wait_ge(lo_ready, N_DN + c + 1)
                pe.wait_ge(a_lo, c + 1)

            by_blocks(N_DN, FT - DN_TAIL, DN_TAIL, hidden, DN_BANKS, wait_down, lambda t, c: None, False)


def rope_table():
    half = HD // 2
    freq = (np.float32(10000.0) ** (-np.arange(half, dtype=np.float32) / np.float32(half))).astype(np.float32)
    ang = (np.arange(SEQ, dtype=np.float32)[None, :] * freq[:, None]).astype(np.float32)
    cos, sin = np.cos(ang).astype(np.float32), np.sin(ang).astype(np.float32)
    return np.ascontiguousarray(np.stack([np.concatenate([cos] * 4), np.concatenate([-sin, sin] * 2)], axis=1))


def rope_table_by_token():
    half = HD // 2
    freq = (np.float32(10000.0) ** (-np.arange(half, dtype=np.float32) / np.float32(half))).astype(np.float32)
    ang = (np.arange(SEQ, dtype=np.float32)[:, None] * freq[None, :]).astype(np.float32)
    table = np.stack([np.cos(ang), np.sin(ang)], axis=1).astype(np.float32)
    return np.ascontiguousarray(table.reshape(TB, P, 2, half).transpose(1, 0, 2, 3))


def head_selector():
    return (np.arange(32)[:, None] % HEADS == np.arange(HEADS)[None, :]).astype(np.float32)


def lay_out_slabs(w_in, w_o_fox, w_o_swa, w_out, w_gate, w_up, w_down):
    cols = np.cumsum([FOX_W, FOX_W, FOX_W, HEADS, FOX_W, KV_W, KV_W, D, D])
    qf, kf, vf, fl, qs, ks, vs, gf, gs = np.split(w_in, cols[:-1], axis=1)

    def by_columns(w):
        n = w.shape[1] // P
        return w.reshape(KC, P, n, P).transpose(2, 1, 0, 3).reshape(n, P, D)

    qs = qs.reshape(D, 2, 4, HD).transpose(0, 2, 1, 3).reshape(D, FOX_W)
    os_ = w_o_swa.reshape(2, 4, HD, D).transpose(1, 0, 2, 3).reshape(FOX_W, D)
    qs = by_columns(qs)
    v = vf.reshape(4, 2, P, FOX_W).transpose(0, 2, 1, 3).reshape(4, P, D)
    gates = np.stack([by_columns(gf), by_columns(gs)], axis=1).reshape(16, P, D)
    wo = by_columns(np.concatenate([w_o_fox, os_]))
    ff = np.stack([by_columns(w_gate), by_columns(w_up)], axis=1).reshape(2 * FT, P, D)
    slabs = np.concatenate([qs, by_columns(qf), by_columns(kf), v, gates, wo,
                            w_out.reshape(KC, P, D), ff, w_down.reshape(FT, P, D)])
    vk = np.concatenate([vs, ks, fl], axis=1).reshape(2, KC // 2, P, VK_W).transpose(0, 2, 1, 3)
    vk = vk.reshape(2, P, KC // 2 * VK_W)
    return np.ascontiguousarray(slabs), np.ascontiguousarray(vk)


def kernel(**inputs):
    import concourse.bacc as bacc
    from concourse.bass_utils import run_bass_kernel_spmd

    a = {k: np.asarray(v) for k, v in inputs.items()}
    slabs, vk = lay_out_slabs(*(a[k][0] for k in ("w_in", "w_o_fox", "w_o_swa", "w_out", "w_gate", "w_up", "w_down")))
    arrays = {
        "xT": np.ascontiguousarray(a["x"][0].T.reshape(KC, P, SEQ)),
        "x": np.ascontiguousarray(a["x"][0]),
        "slabs": slabs,
        "vk_slabs": vk,
        "rope": rope_table(),
        "rope_tok": rope_table_by_token(),
        "sel": head_selector(),
        "b_forget": np.ascontiguousarray(a["b_forget"][0]),
        "sinks": np.ascontiguousarray(a["attn_sinks"][0]),
        "ln1_g": np.ascontiguousarray(a["ln1_g"][0]),
        "ln1_b": np.ascontiguousarray(a["ln1_b"][0]),
        "ln2_g": np.ascontiguousarray(a["ln2_g"][0]),
        "ln2_b": np.ascontiguousarray(a["ln2_b"][0]),
    }
    nc = bacc.Bacc("TRN2", target_bir_lowering=False, num_devices=1)
    args = [nc.dram_tensor(f"in_{k}", v.shape, mybir.dt.from_np(v.dtype), kind="ExternalInput").ap()
            for k, v in arrays.items()]
    out = nc.dram_tensor("out_0", (SEQ, D), F32, kind="ExternalOutput").ap()
    program(nc, *args, out)
    r = run_bass_kernel_spmd(nc, [{f"in_{k}": v for k, v in arrays.items()}], core_ids=[0])
    return r.results[0]["out_0"].reshape(1, SEQ, D)
```
